# Optimizing a Trainium2 kernel written in Bass

```python
import jax, jax.numpy as jnp
from jax import lax
import numpy as np

'''One inference step of a 2-layer hybrid streaming encoder trunk (Hymba-style parallel head groups).

Each layer: x -> RMSNorm -> ONE combined input projection whose columns are split between
  * head group A: gated linear attention (GLA, 4 heads, key dim 64, value dim 128, low-rank
    data-dependent forget gate, per-token causal recurrence computed in 64-frame chunks), and
  * head group B: stick-breaking attention (8 heads of dim 64, QK-norm, no positional encoding,
    strictly causal, swept in 128-query blocks),
the two group outputs are concatenated and sent through ONE output projection (residual add),
then RMSNorm -> squared-ReLU MLP (hidden 4*D_MODEL) -> residual add.

Inputs:
  x_prompt     (BATCH, SEQ, D_MODEL)          first SEQ frames of BATCH new streams
  x_sample     (DEC_BATCH, DEC_SEQ, D_MODEL)  next DEC_SEQ frames of DEC_BATCH running streams
  cache_sb_k   (DEPTH, DEC_BATCH, PAST_LEN, SB_HEADS, SB_HD)  QK-normed stick-breaking keys of past frames
  cache_sb_v   (DEPTH, DEC_BATCH, PAST_LEN, SB_HEADS, SB_HD)  stick-breaking values of past frames
  state_gla    (DEPTH, DEC_BATCH, GLA_HEADS, GLA_DK, GLA_DV)  GLA recurrent state after the past frames
  weights stacked over DEPTH (see setup_inputs).

Returns the tuple
  (y_prompt        (BATCH, SEQ, D_MODEL),
   y_sample        (DEC_BATCH, DEC_SEQ, D_MODEL),
   new_sb_k_prompt (DEPTH, BATCH, SEQ, SB_HEADS, SB_HD),
   new_sb_v_prompt (DEPTH, BATCH, SEQ, SB_HEADS, SB_HD),
   new_gla_prompt  (DEPTH, BATCH, GLA_HEADS, GLA_DK, GLA_DV),
   new_sb_k_sample (DEPTH, DEC_BATCH, DEC_SEQ, SB_HEADS, SB_HD),
   new_sb_v_sample (DEPTH, DEC_BATCH, DEC_SEQ, SB_HEADS, SB_HD),
   new_gla_sample  (DEPTH, DEC_BATCH, GLA_HEADS, GLA_DK, GLA_DV))
'''

D_MODEL = 1024
BATCH = 1
SEQ = 2048
DEPTH = 1
DEC_BATCH = 1
DEC_SEQ = 64
PAST_LEN = 512

CHUNK = 64
Q_BLOCK = 128
MIX_WIDTH = D_MODEL
GLA_WIDTH = MIX_WIDTH // 2
GLA_HEADS = 4
GLA_DV = GLA_WIDTH // GLA_HEADS
GLA_DK = GLA_DV // 2
GLA_KEY = GLA_HEADS * GLA_DK
GATE_RANK = 16
GATE_NORM = 16.0
SB_WIDTH = MIX_WIDTH - GLA_WIDTH
SB_HEADS = 8
SB_HD = SB_WIDTH // SB_HEADS
D_FF = 4 * D_MODEL
EPS = 1e-6
SPLITS = (GLA_KEY, GLA_KEY, GLA_WIDTH, GLA_WIDTH, GATE_RANK, SB_WIDTH, SB_WIDTH, SB_WIDTH)
IN_COLS = sum(SPLITS)
SPLIT_IDX = [int(i) for i in np.cumsum(SPLITS)[:-1]]

kernel_name = 'gla_stickbreaking_hybrid_stream_step'

def rmsnorm(x, g):
    xf = x.astype(jnp.float32)
    return xf * lax.rsqrt(jnp.mean(xf * xf, axis=-1, keepdims=True) + EPS) * g.astype(jnp.float32)

def project(x, norm_g, w_in, w_a2, b_a2, q_g, k_g):
    B, T = x.shape[0], x.shape[1]
    xn = rmsnorm(x, norm_g).astype(x.dtype)
    proj = (xn @ w_in).astype(jnp.float32)
    gq, gk, gv, gate, alr, sq, sk, sv = jnp.split(proj, SPLIT_IDX, axis=-1)
    log_a = jax.nn.log_sigmoid(alr @ w_a2.astype(jnp.float32) + b_a2.astype(jnp.float32)) / GATE_NORM

    def heads(t, h):
        return t.reshape(B, T, h, -1).transpose(0, 2, 1, 3)

    gla = (heads(gq, GLA_HEADS) * GLA_DK ** -0.5, heads(gk, GLA_HEADS), heads(gv, GLA_HEADS), heads(log_a, GLA_HEADS))
    sb = (rmsnorm(sq.reshape(B, T, SB_HEADS, SB_HD), q_g),
          rmsnorm(sk.reshape(B, T, SB_HEADS, SB_HD), k_g),
          sv.reshape(B, T, SB_HEADS, SB_HD))
    return gla, sb, gate

def gla_chunk(S, inp):
    q, k, v, la = inp
    L = q.shape[2]
    b = jnp.cumsum(la, axis=2)
    causal = jnp.tril(jnp.ones((L, L), dtype=bool))
    diff = b[:, :, :, None, :] - b[:, :, None, :, :]
    decay = jnp.exp(jnp.where(causal[None, None, :, :, None], diff, -jnp.inf))
    scores = jnp.einsum('bhtd,bhsd,bhtsd->bhts', q, k, decay)
    o = jnp.einsum('bhts,bhsv->bhtv', scores, v) + jnp.einsum('bhtd,bhdv->bhtv', q * jnp.exp(b), S)
    b_end = b[:, :, -1:, :]
    S_new = jnp.exp(b_end[:, :, 0, :])[..., None] * S + jnp.einsum('bhsd,bhsv->bhdv', k * jnp.exp(b_end - b), v)
    return S_new, o

def gla_prompt(q, k, v, la):
    B, H, T, _ = q.shape
    n = T // CHUNK

    def chunks(t):
        return jnp.moveaxis(t.reshape(B, H, n, CHUNK, t.shape[-1]), 2, 0)

    S0 = jnp.zeros((B, H, GLA_DK, GLA_DV), jnp.float32)
    S, o = lax.scan(gla_chunk, S0, (chunks(q), chunks(k), chunks(v), chunks(la)))
    o = jnp.moveaxis(o, 0, 2).reshape(B, H, T, GLA_DV)
    return S, o

def sb_block(q, q_pos, k, v, k_pos):
    z = jnp.einsum('bqhd,bkhd->bhqk', q, k) * SB_HD ** -0.5
    mask = (k_pos[None, :] < q_pos[:, None])[None, None]
    log_beta = jax.nn.log_sigmoid(z)
    l = jnp.where(mask, jax.nn.log_sigmoid(-z), 0.0)
    c = lax.cumsum(l, axis=3, reverse=True) - l
    w = jnp.where(mask, jnp.exp(log_beta + c), 0.0)
    return jnp.einsum('bhqk,bkhd->bqhd', w, v)

def sb_prompt(q, k, v):
    B, T, H, d = q.shape
    nb = T // Q_BLOCK
    pos = jnp.arange(T)
    qb = jnp.moveaxis(q.reshape(B, nb, Q_BLOCK, H, d), 1, 0)
    starts = jnp.arange(nb) * Q_BLOCK
    out = lax.map(lambda a: sb_block(a[0], a[1] + jnp.arange(Q_BLOCK), k, v, pos), (qb, starts))
    return jnp.moveaxis(out, 0, 1).reshape(B, T, H, d)

def finish(x, o_gla, gate, o_sb, gla_norm_g, w_out, norm2_g, w_up, w_down):
    B, T = x.shape[0], x.shape[1]
    og = rmsnorm(o_gla, gla_norm_g).transpose(0, 2, 1, 3).reshape(B, T, GLA_WIDTH) * jax.nn.silu(gate)
    mix = jnp.concatenate([og, o_sb.reshape(B, T, SB_WIDTH)], axis=-1).astype(x.dtype)
    h = x + mix @ w_out
    u = rmsnorm(h, norm2_g).astype(x.dtype) @ w_up
    return h + jnp.square(jax.nn.relu(u)) @ w_down

def setup_inputs(seed: int = 0) -> dict:
    key = jax.random.key(seed)
    ks = jax.random.split(key, 20)
    f32 = jnp.float32
    nrm = lambda k, s, sc: jax.random.normal(k, s, f32) * sc
    return {
        'x_prompt': nrm(ks[0], (BATCH, SEQ, D_MODEL), 1.0),
        'x_sample': nrm(ks[1], (DEC_BATCH, DEC_SEQ, D_MODEL), 1.0),
        'cache_sb_k': nrm(ks[2], (DEPTH, DEC_BATCH, PAST_LEN, SB_HEADS, SB_HD), 1.0),
        'cache_sb_v': nrm(ks[3], (DEPTH, DEC_BATCH, PAST_LEN, SB_HEADS, SB_HD), 1.0),
        'state_gla': nrm(ks[4], (DEPTH, DEC_BATCH, GLA_HEADS, GLA_DK, GLA_DV), 0.5),
        'norm1_g': 1.0 + nrm(ks[5], (DEPTH, D_MODEL), 0.02),
        'w_in': nrm(ks[6], (DEPTH, D_MODEL, IN_COLS), D_MODEL ** -0.5),
        'w_a2': nrm(ks[7], (DEPTH, GATE_RANK, GLA_KEY), GATE_RANK ** -0.5),
        'b_a2': nrm(ks[8], (DEPTH, GLA_KEY), 0.1),
        'q_norm_g': 1.0 + nrm(ks[9], (DEPTH, SB_HD), 0.02),
        'k_norm_g': 1.0 + nrm(ks[10], (DEPTH, SB_HD), 0.02),
        'gla_norm_g': 1.0 + nrm(ks[11], (DEPTH, GLA_DV), 0.02),
        'w_out': nrm(ks[12], (DEPTH, MIX_WIDTH, D_MODEL), MIX_WIDTH ** -0.5),
        'norm2_g': 1.0 + nrm(ks[13], (DEPTH, D_MODEL), 0.02),
        'w_up': nrm(ks[14], (DEPTH, D_MODEL, D_FF), D_MODEL ** -0.5),
        'w_down': nrm(ks[15], (DEPTH, D_FF, D_MODEL), D_FF ** -0.5),
    }

def reference(x_prompt, x_sample, cache_sb_k, cache_sb_v, state_gla, norm1_g, w_in, w_a2, b_a2,
              q_norm_g, k_norm_g, gla_norm_g, w_out, norm2_g, w_up, w_down):
    dt = x_prompt.dtype
    xp, xs = x_prompt, x_sample
    kp_l, vp_l, sp_l, ks_l, vs_l, ss_l = [], [], [], [], [], []
    P = cache_sb_k.shape[2]
    for l in range(DEPTH):
        lw = (norm1_g[l], w_in[l], w_a2[l], b_a2[l], q_norm_g[l], k_norm_g[l])
        tail = (gla_norm_g[l], w_out[l], norm2_g[l], w_up[l], w_down[l])
        gla_in, (sq, sk, sv), gate = project(xp, *lw)
        S_p, o_g = gla_prompt(*gla_in)
        o_s = sb_prompt(sq, sk, sv)
        xp = finish(xp, o_g, gate, o_s, *tail)
        kp_l.append(sk.astype(dt))
        vp_l.append(sv.astype(dt))
        sp_l.append(S_p.astype(dt))
        T = xs.shape[1]
        gla_in, (sq, sk, sv), gate = project(xs, *lw)
        S_s, o_g = gla_chunk(state_gla[l].astype(jnp.float32), gla_in)
        k_all = jnp.concatenate([cache_sb_k[l].astype(jnp.float32), sk], axis=1)
        v_all = jnp.concatenate([cache_sb_v[l].astype(jnp.float32), sv], axis=1)
        o_s = sb_block(sq, P + jnp.arange(T), k_all, v_all, jnp.arange(P + T))
        xs = finish(xs, o_g, gate, o_s, *tail)
        ks_l.append(sk.astype(dt))
        vs_l.append(sv.astype(dt))
        ss_l.append(S_s.astype(dt))
    return (xp, xs, jnp.stack(kp_l), jnp.stack(vp_l), jnp.stack(sp_l), jnp.stack(ks_l), jnp.stack(vs_l), jnp.stack(ss_l))


_drawn_inputs = setup_inputs


def setup_inputs(seed=0):
    import zlib

    import numpy as np

    out = dict(_drawn_inputs(seed))
    spreads = {}
    factors = {'q_norm_g': 52.858, 'gla_norm_g': 6.638, 'norm2_g': 3.265}
    for name, (base, spread) in spreads.items():
        noise = np.random.default_rng([zlib.crc32(name.encode()), seed]).standard_normal(out[name].shape)
        drawn = base * np.exp(spread * noise) if base else spread * noise
        out[name] = __import__('jax').numpy.asarray(drawn.astype(out[name].dtype))
    for name, factor in factors.items():
        out[name] = (out[name] * factor).astype(out[name].dtype)
    return out
```

```python
from contextlib import ExitStack

import concourse.bass as bass
from concourse import mybir

F32 = mybir.dt.float32
F32R = mybir.dt.float32r
ALU = mybir.AluOpType
ACT = mybir.ActivationFunctionType
AX = mybir.AxisListType

P = 128
D = 1024
KC = D // P
SEQ, DEC, PAST = 2048, 64, 512
TILES = SEQ // P + 1
ROWS = TILES * P
KEYS = SEQ + PAST + P
NEW_KEY_COL = SEQ + PAST
GLA_HEADS, DK, DV = 4, 64, 128
SB_HEADS, HD = 8, 64
RANK = 16
GATE_NORM = 16.0
D_FF = 4 * D
EPS = 1e-6
NEG = -(2.0 ** 100)
CHUNK = 64
LEVELS = (32, 16, 8, 4, 2, 1)

C_GQK, C_GV, C_GATE, C_ALR, C_SQ, C_SK, C_SV = 0, 512, 1024, 1536, 1552, 2064, 2576
GROUP_COLS = (C_SQ, C_SK, C_SV, C_GQK, C_GV, C_GATE)
NG = len(GROUP_COLS)
FULL_BLOCKS = 3
BT = 4
LAST_BT = TILES - FULL_BLOCKS * BT


class Pool:

    def __init__(self, nc, tag):
        self.nc, self.tag, self.ctx, self.semaphores = nc, tag, ExitStack(), []

    def __enter__(self):
        return self

    def __exit__(self, *a):
        done = self.ctx.__exit__(*a)
        self.nc.clear_and_free_semaphores(self.semaphores)
        self.nc.all_engine_barrier()
        return done

    def sb(self, name, shape, dt=F32):
        return self.ctx.enter_context(self.nc.sbuf_tensor(f"{self.tag}_{name}", shape, dt))

    def ps(self, name, shape, dt=F32):
        return self.ctx.enter_context(self.nc.psum_tensor(f"{self.tag}_{name}", shape, dt))

    def sem(self, name):
        self.semaphores.append(self.nc.alloc_semaphore(f"{self.tag}_{name}"))
        return self.semaphores[-1]

    def sems(self, name, n):
        return [self.sem(f"{name}{i}") for i in range(n)]

    def block(self):
        return self.ctx.enter_context(self.nc.Block())


def raw(ap):
    return ap.bitcast(F32)


def stop_at(eng, sem, value, passed):
    eng.wait_ge(sem, value)
    eng.sem_inc(passed, 1)


def bcast_rows(ap, n):
    return bass.AP(tensor=ap.tensor, offset=ap.offset, ap=[[0, P], [1, n]])


def rows(ap, t, n=1):
    return ap[bass.ds(t * P, n * P), :]


def blocks_loop(eng, body):
    with eng.Fori(0, FULL_BLOCKS) as b:
        body(b, BT, False)
    body(FULL_BLOCKS, LAST_BT, True)


def phase_cache(nc, cache_k, cache_v, ident, kT, vS):
    nt = PAST // P
    with Pool(nc, "cc") as m:
        idt = m.sb("idt", [P, P])
        k_in = m.sb("k_in", [P, nt, SB_HEADS, HD])
        v_in = m.sb("v_in", [P, nt, SB_HEADS, HD])
        ks = m.sb("ks", [P, nt, SB_HEADS, 2, HD], F32R)
        vs = m.sb("vs", [P, nt, SB_HEADS, 2, HD], F32R)
        kts = m.sb("kts", [P, SB_HEADS, nt, P], F32R)
        tp = m.ps("tp", [P, 2, 4, P])
        s_id, s_kin, s_vin = m.sem("id"), m.sem("kin"), m.sem("vin")
        s_kh, s_vh, s_kl, s_vl = m.sem("kh"), m.sem("vh"), m.sem("kl"), m.sem("vl")
        s_tp, s_ev, s_out = m.sem("tp"), m.sem("ev"), m.sem("out")
        block = m.block()

        @block.sync
        def _(sp):
            sp.dma_start(idt[:], ident).then_inc(s_id, 16)
            sp.dma_start(k_in[:], cache_k.rearrange("(t p) h d -> p t h d", p=P)).then_inc(s_kin, 16)
            sp.dma_start(v_in[:], cache_v.rearrange("(t p) h d -> p t h d", p=P)).then_inc(s_vin, 16)
            sp.wait_ge(s_vl, 1)
            sp.dma_start(vS[SEQ:SEQ + PAST, :].rearrange("(t p) c -> p t c", p=P),
                         raw(vs[:]).rearrange("p t h a d -> p t (h a d)")).then_inc(s_out, 16)
            sp.wait_ge(s_ev, nt * 2)
            for h in range(SB_HEADS):
                sp.dma_start(kT[h, :, SEQ:SEQ + PAST], raw(kts[:, h]).rearrange("p t k -> p (t k)")).then_inc(s_out, 16)
            sp.wait_ge(s_out, 16 * (1 + SB_HEADS))

        @block.scalar
        def _(act):
            act.wait_ge(s_kin, 16)
            act.activation(ks[:, :, :, 0, :], k_in[:], ACT.Copy).then_inc(s_kh, 1)
            act.wait_ge(s_vin, 16)
            act.activation(vs[:, :, :, 0, :], v_in[:], ACT.Copy).then_inc(s_vh, 1)
            for n in range(nt * 2):
                act.wait_ge(s_tp, n + 1)
                t, g = n // 2, n % 2
                act.activation(kts[:, 4 * g:4 * g + 4, t, :], tp[:, n % 2], ACT.Copy).then_inc(s_ev, 1)

        @block.vector
        def _(dve):
            dve.wait_ge(s_kh, 1)
            dve.tensor_tensor(ks[:, :, :, 1, :], k_in[:], raw(ks[:, :, :, 0, :]), ALU.subtract).then_inc(s_kl, 1)
            dve.wait_ge(s_vh, 1)
            dve.tensor_tensor(vs[:, :, :, 1, :], v_in[:], raw(vs[:, :, :, 0, :]), ALU.subtract).then_inc(s_vl, 1)

        @block.tensor
        def _(pe):
            pe.wait_ge(s_id, 16)
            pe.wait_ge(s_kl, 1)
            for n in range(nt * 2):
                t, g = n // 2, n % 2
                if n >= 2:
                    pe.wait_ge(s_ev, n - 1)
                for h in range(4):
                    src = raw(ks[:, t, 4 * g + h]).rearrange("p a d -> p (a d)")
                    last = pe.transpose(tp[:, n % 2, h, :], src, idt[:])
                last.then_inc(s_tp, 1)


def phase_project(nc, x, norm_g, w_in, w_a2, b_a2, qg, kg, ident, qT, kT, vS, new_k, new_v, gqk, gv, sgate, la):
    with Pool(nc, "pj") as m:
        idt = m.sb("idt", [P, P])
        gb = m.sb("gb", [P, D])
        g64 = m.sb("g64", [P, 2, HD])
        wa2 = m.sb("wa2", [32, 256])
        half_pow = m.sb("half_pow", [P, SB_HEADS])
        xb = m.sb("xb", [P, 2, D])
        xn = m.sb("xn", [P, 2, D])
        ssx = m.sb("ssx", [P, 2, 3])
        xh = m.sb("xh", [P, KC, LAST_BT * P], F32R)
        xl = m.sb("xl", [P, KC, LAST_BT * P], F32R)
        wr = m.sb("wr", [P, KC, 512])
        wh = m.sb("wh", [P, 2, KC, 512], F32R)
        wl = m.sb("wl", [P, 2, KC, 512], F32R)
        wah = m.sb("wah", [P, KC, P], F32R)
        wal = m.sb("wal", [P, KC, P], F32R)
        alrT = m.sb("alrT", [32, LAST_BT * P])
        lt = m.sb("lt", [P, 2, 256])
        ld = m.sb("ld", [P, 2, 256])
        tmp = m.sb("tmp", [P, 2, 512])
        ss8 = m.sb("ss8", [P, 2, SB_HEADS])
        ms8 = m.sb("ms8", [P, 2, SB_HEADS])
        r8 = m.sb("r8", [P, 2, SB_HEADS])
        nq = m.sb("nq", [P, 2, 512])
        kn = m.sb("kn", [P, 2, 512])
        vn = m.sb("vn", [P, 2, 512])
        stk = m.sb("stk", [P, 2, SB_HEADS, 2, HD], F32R)
        vst = m.sb("vst", [P, 2, SB_HEADS, 2, HD], F32R)
        stT = m.sb("stT", [P, 2, SB_HEADS, P], F32R)
        ng = m.sb("ng", [P, 2, 512])
        ge = m.sb("ge", [P, 2, 512])
        war = tmp[:].rearrange("p a (c n) -> p (a c) n", n=P)
        pj = m.ps("pj", [P, 4, 512])
        tx = m.ps("tx", [P, 2, 512])
        tT = m.ps("tT", [P, 2, 512])

        s_c, s_cs = m.sem("consts"), m.sem("consts_set")
        s_x, s_sq, s_r1, s_rx, s_xn = m.sems("x", 2), m.sem("sq"), m.sem("r1"), m.sem("rx"), m.sem("xn")
        s_tx, s_txf, s_xh = m.sem("tx"), m.sem("txf"), m.sem("xh")
        s_wa, s_wah, s_wal = m.sem("wa"), m.sem("wah"), m.sem("wal")
        s_wr, s_wh, s_wl = m.sem("wr"), m.sem("wh"), m.sem("wl")
        s_ae, s_la = m.sem("ae"), m.sems("la", 2)
        s_pj, s_bank = m.sem("pj"), m.sem("bank")
        s_qs, s_qr, s_qp, s_qq, s_qg, s_qh, s_ql, s_tT, s_ev = [m.sem(n) for n in
            ("qs", "qr", "qp", "qq", "qg", "qh", "ql", "tT", "ev")]
        s_kd, s_sd = m.sems("kd", 2), m.sems("sd", 2)
        s_vh, s_vd, s_vsd = m.sem("vh"), m.sems("vd", 2), m.sems("vsd", 2)
        s_pass, s_passed = m.sem("pass"), m.sem("passed")
        s_ge, s_gp, s_gr, s_ngd = m.sem("ge"), m.sem("gp"), m.sem("gr"), m.sems("ngd", 2)
        block = m.block()

        Q_, K_, V_, GATE_ = 0, 1, 2, 5
        TX_USES = 3 * BT + 2
        BANKS, RING = 4, 2

        def slots(nt):
            return [(g, j) for g in range(NG) for j in range(nt)]

        @block.sync
        def _(sp):
            sp.dma_start(idt[:], ident).then_inc(s_c, 16)
            sp.dma_start(gb[:], bcast_rows(norm_g, D)).then_inc(s_c, 16)
            sp.dma_start(g64[:, 0], bcast_rows(qg, HD)).then_inc(s_c, 16)
            sp.dma_start(g64[:, 1], bcast_rows(kg, HD)).then_inc(s_c, 16)
            sp.dma_start(wa2[0:RANK, :], w_a2).then_inc(s_c, 16)
            sp.dma_start(wa2[RANK:RANK + 1, :], b_a2).then_inc(s_c, 16)

            def load_x(b, j):
                sp.wait_ge(s_xn, b * BT + j + 1)
                sp.dma_start(xb[:, j % 2], rows(x, b * BT + j)).then_inc(s_x[j % 2], 16)

            def load_w(b, g):
                sp.wait_ge(s_wl, b * NG + g)
                sp.dma_start(wr[:], w_in[:, GROUP_COLS[g]:GROUP_COLS[g] + 512]
                             .rearrange("(c p) n -> p c n", p=P)).then_inc(s_wr, 16)

            load_x(0, 0)
            load_x(0, 1)
            sp.wait_ge(s_cs, 3)
            sp.dma_start(war[:, :, 0:RANK], w_in[:, C_ALR:C_ALR + RANK].rearrange("(c p) n -> p c n", p=P)).then_inc(s_wa, 16)
            load_w(0, 0)

            def body(b, nt, last):
                for j in range(2, nt):
                    load_x(b, j)
                for j in range(nt):
                    sp.wait_ge(s_txf, b * TX_USES + 2 * nt + 2 + j + 1 + RING)
                    sp.dma_start(rows(la, b * BT + j), ld[:, j % 2]).then_inc(s_la[j % 2], 16)
                items = slots(nt)
                for n in range(len(items) + 2):
                    if n < len(items) and items[n][1] == 0:
                        g = items[n][0]
                        if g + 1 < NG:
                            load_w(b, g + 1)
                        elif not last:
                            load_w(b + 1, 0)
                            load_x(b + 1, 0)
                            load_x(b + 1, 1)
                    if 1 <= n <= len(items):
                        g, j = items[n - 1]
                        sample = last and j == nt - 1
                        row = b * BT + j
                        drained = b * NG * BT + n + BANKS
                        if g == K_:
                            sp.wait_ge(s_qg, b * 2 * BT + nt + j + 1)
                            sp.dma_start(new_k[SEQ:SEQ + DEC, :] if sample else rows(new_k, row),
                                         kn[0:DEC, j % 2] if sample else kn[:, j % 2]).then_inc(s_kd[j % 2], 16)
                        elif g == V_:
                            sp.wait_ge(s_bank, drained)
                            sp.dma_start(new_v[SEQ:SEQ + DEC, :] if sample else rows(new_v, row),
                                         vn[0:DEC, j % 2] if sample else vn[:, j % 2]).then_inc(s_vd[j % 2], 16)
                            key = NEW_KEY_COL if sample else row * P
                            sp.dma_start(vS[bass.ds(key, P), :], raw(vst[:, j % 2]).rearrange("p h a d -> p (h a d)")).then_inc(s_vsd[j % 2], 16)
                        elif g > V_:
                            q = (g - 3) * nt + j
                            sp.wait_ge(s_bank, drained)
                            sp.dma_start(rows((gqk, gv, sgate)[g - 3], row), ng[:, q % 2]).then_inc(s_ngd[q % 2], 16)
                    if n >= 2:
                        g, j = items[n - 2]
                        if g <= K_:
                            q = g * nt + j
                            stop_at(sp, s_ev, (b * 2 * BT + q + 1) * 2 + RING, s_passed)
                            col = NEW_KEY_COL if g == K_ and last and j == nt - 1 else (b * BT + j) * P
                            sp.dma_start((qT, kT)[g][:, :, bass.ds(col, P)].rearrange("h p k -> p h k"),
                                         raw(stT[:, q % 2])).then_inc(s_sd[q % 2], 16)

            blocks_loop(sp, body)
            for q in range(2):
                for s, per_tile in ((s_la, 1), (s_kd, 1), (s_vd, 1), (s_vsd, 1), (s_sd, 2), (s_ngd, 3)):
                    sp.wait_ge(s[q], 16 * ((per_tile * TILES + 1 - q) // 2))

        @block.gpsimd
        def _(pool):
            pool.memset(half_pow[:], -0.5).then_inc(s_cs, 1)
            pool.memset(war, 0.0).then_inc(s_cs, 1)
            pool.memset(alrT[:], 1.0).then_inc(s_cs, 1)
            pool.wait_ge(s_c, 96)
            pool.tensor_scalar(g64[:, 0], g64[:, 0], HD ** -0.5, 1.0, ALU.mult, ALU.mult).then_inc(s_cs, 1)
            pool.wait_ge(s_cs, 4)
            pool.wait_ge(s_wah, 1)
            pool.tensor_tensor(wal[:], war, raw(wah[:]), ALU.subtract).then_inc(s_wal, 1)

            def split_w(b, g):
                pool.wait_ge(s_wh, b * NG + g + 1)
                pool.tensor_tensor(wl[:, g % 2], wr[:], raw(wh[:, g % 2]), ALU.subtract).then_inc(s_wl, 1)

            split_w(0, 0)

            def body(b, nt, last):
                for j in range(nt):
                    t = b * BT + j
                    stop_at(pool, s_sq, t + 1, s_pass)
                    pool.tensor_scalar(ssx[:, j % 2, 1:2], ssx[:, j % 2, 0:1], 1.0 / D, EPS, ALU.mult, ALU.add).then_inc(s_r1, 1)
                    pool.wait_ge(s_r1, t + 1)
                    pool.tensor_tensor(ssx[:, j % 2, 2:3], ssx[:, j % 2, 1:2], half_pow[:, 0:1], ALU.pow).then_inc(s_rx, 1)
                items = slots(nt)
                for n in range(len(items) + 1):
                    if n < len(items):
                        g, j = items[n]
                        if g <= K_:
                            q = g * nt + j
                            c = b * 2 * BT + q
                            stop_at(pool, s_qr, c + 1 + RING, s_pass)
                            pool.tensor_scalar(ms8[:, q % 2], ss8[:, q % 2], 1.0 / HD, EPS, ALU.mult, ALU.add).then_inc(s_qp, 1)
                            pool.wait_ge(s_qp, c + 1)
                            pool.tensor_tensor(r8[:, q % 2], ms8[:, q % 2], half_pow[:], ALU.pow).then_inc(s_qq, 1)
                        elif g == GATE_:
                            stop_at(pool, s_ge, b * BT + j + 1, s_pass)
                            pool.tensor_scalar(ge[:, j % 2], ge[:, j % 2], 1.0, 1.0, ALU.add, ALU.mult).then_inc(s_gp, 1)
                    if n >= 1:
                        g, j = items[n - 1]
                        if g <= K_:
                            q = g * nt + j
                            c = b * 2 * BT + q
                            pool.wait_ge(s_bank, b * NG * BT + n + BANKS)
                            out = nq
                            if g == K_:
                                out = kn
                                pool.wait_ge(s_kd[j % 2], 16 * (b * BT // 2 + j // 2))
                                pool.wait_ge(s_ql, c - 1)
                                assert nt + j - 1 > 0
                            oo = out[:, (j if g == K_ else q) % 2].rearrange("p (h d) -> p h d", d=HD)
                            pool.tensor_tensor(oo, nq[:, q % 2].rearrange("p (h d) -> p h d", d=HD),
                                               g64[:, g:g + 1].to_broadcast([P, SB_HEADS, HD]), ALU.mult).then_inc(s_qg, 1)
                    if n < len(items) and items[n][1] == 1:
                        g = items[n][0]
                        if g + 1 < NG:
                            split_w(b, g + 1)
                        elif not last:
                            split_w(b + 1, 0)

            blocks_loop(pool, body)

        @block.scalar
        def _(act):
            act.preload_act_table_set("natural_log_exp_and_others")
            act.wait_ge(s_wa, 16)
            act.activation(wah[:], war, ACT.Copy).then_inc(s_wah, 1)

            def split_w(b, g, nt):
                act.wait_ge(s_wr, 16 * (b * NG + g + 1))
                act.wait_ge(s_pj, b * NG * BT + ((g - 1) * nt + BT if g > 1 else g * BT))
                act.activation(wh[:, g % 2], wr[:], ACT.Copy).then_inc(s_wh, 1)

            split_w(0, 0, BT)
            act.wait_ge(s_wal, 1)

            def square(b, j):
                t = b * BT + j
                act.wait_ge(s_x[j % 2], 16 * (b * BT // 2 + j // 2 + 1))
                if j >= 2:
                    act.wait_ge(s_tx, b * TX_USES + 2 * (j - 1))
                else:
                    act.wait_ge(s_tx, b * TX_USES)
                act.activation(xn[:, j % 2], xb[:, j % 2], ACT.Square, accum_out=ssx[:, j % 2, 0:1]).then_inc(s_sq, 1)

            def body(b, nt, last):
                square(b, 0)
                for j in range(nt):
                    if j + 1 < nt:
                        square(b, j + 1)
                    if j == 0:
                        act.wait_ge(s_pj, b * NG * BT + BT)
                    for a in range(2):
                        act.wait_ge(s_tx, b * TX_USES + 2 * j + a + 1)
                        act.activation(xh[:, 4 * a:4 * a + 4, j * P:(j + 1) * P],
                                       tx[:, a].rearrange("p (c k) -> p c k", k=P), ACT.Copy).then_inc(s_xh, 1)
                for j in range(nt):
                    t = b * BT + j
                    act.wait_ge(s_tx, b * TX_USES + 2 * nt + 2 + j + 1)
                    if j >= 2:
                        act.wait_ge(s_txf, b * TX_USES + 2 * nt + 2 + j - 1 + RING)
                    act.activation(lt[:, j % 2], tx[:, j % 2, 0:256], ACT.Abs).then_inc(s_ae, 1)
                    act.wait_ge(s_ae, 3 * t + 1)
                    act.activation(lt[:, j % 2], lt[:, j % 2], ACT.Exp, scale=-1.0).then_inc(s_ae, 1)
                    act.wait_ge(s_ae, 3 * t + 2)
                    act.activation(lt[:, j % 2], lt[:, j % 2], ACT.Ln, bias=1.0).then_inc(s_ae, 1)
                items = slots(nt)
                for n in range(len(items) + 2):
                    if n < len(items):
                        g, j = items[n]
                        bank = pj[:, n % 4]
                        if g <= K_ or g in (V_, GATE_):
                            act.wait_ge(s_pj, b * NG * BT + n + 1 + BT)
                        if g <= K_:
                            q = g * nt + j
                            act.wait_ge(s_qr, b * 2 * BT + q + 1)
                            act.activation(tmp[:, q % 2], bank, ACT.Square).then_inc(s_qs, 1)
                        elif g == V_:
                            act.wait_ge(s_vd[j % 2], 16 * (b * BT // 2 + j // 2))
                            act.activation(vn[:, j % 2], bank, ACT.Copy)
                            act.wait_ge(s_vsd[j % 2], 16 * (b * BT // 2 + j // 2))
                            act.activation(vst[:, j % 2, :, 0, :], bank.rearrange("p (h d) -> p h d", d=HD),
                                           ACT.Copy).then_inc(s_vh, 1)
                        elif g == GATE_:
                            act.wait_ge(s_bank, b * NG * BT + n - 1 + BANKS)
                            act.activation(ge[:, j % 2], bank, ACT.Exp, scale=-1.0).then_inc(s_ge, 1)
                    if 1 <= n <= len(items):
                        g, j = items[n - 1]
                        if g <= K_:
                            q = g * nt + j
                            c = b * 2 * BT + q
                            act.wait_ge(s_qg, c + 1)
                            act.wait_ge(s_tT, 2 * c)
                            src = kn[:, j % 2] if g == K_ else nq[:, q % 2]
                            act.activation(stk[:, q % 2, :, 0, :], src.rearrange("p (h d) -> p h d", d=HD),
                                           ACT.Copy).then_inc(s_qh, 1)
                    if n >= 2:
                        g, j = items[n - 2]
                        if g <= K_:
                            q = g * nt + j
                            c = b * 2 * BT + q
                            act.wait_ge(s_sd[q % 2], 16 * (b * BT + q // 2))
                            for a in range(2):
                                act.wait_ge(s_tT, 2 * c + a + 1 + RING)
                                act.activation(stT[:, q % 2, 4 * a:4 * a + 4, :],
                                               tT[:, a].rearrange("p (h k) -> p h k", k=P), ACT.Copy).then_inc(s_ev, 1)
                    if n < len(items) and items[n][1] == 1:
                        g = items[n][0]
                        if g + 1 < NG:
                            split_w(b, g + 1, nt)
                        elif not last:
                            split_w(b + 1, 0, BT)

            act.sem_inc(s_ev, RING)
            blocks_loop(act, body)

        @block.vector
        def _(dve):
            dve.sem_inc(s_xn, RING)
            dve.sem_inc(s_txf, RING)
            dve.sem_inc(s_bank, BANKS)
            dve.sem_inc(s_qr, RING)
            dve.wait_ge(s_c, 96)

            def body(b, nt, last):
                for j in range(nt):
                    t = b * BT + j
                    dve.wait_ge(s_rx, t + 1)
                    dve.scalar_tensor_tensor(out=xn[:, j % 2], in0=xb[:, j % 2], scalar=ssx[:, j % 2, 2:3], in1=gb[:],
                                             op0=ALU.mult, op1=ALU.mult).then_inc(s_xn, 1)
                    for a in range(2):
                        dve.wait_ge(s_xh, 2 * t + a + 1)
                        dst = xh[:, 4 * a:4 * a + 4, j * P:(j + 1) * P]
                        dve.tensor_tensor(xl[:, 4 * a:4 * a + 4, j * P:(j + 1) * P],
                                          tx[:, a].rearrange("p (c k) -> p c k", k=P), raw(dst), ALU.subtract).then_inc(s_txf, 1)
                half = nt * P // 2
                for a in range(2):
                    dve.wait_ge(s_tx, b * TX_USES + 2 * nt + a + 1)
                    dve.tensor_copy(alrT[0:RANK, a * half:(a + 1) * half], tx[0:RANK, a, 0:half]).then_inc(s_txf, 1)
                for j in range(nt):
                    t = b * BT + j
                    dve.wait_ge(s_ae, 3 * t + 3)
                    dve.wait_ge(s_la[j % 2], 16 * (b * BT // 2 + j // 2))
                    dve.scalar_tensor_tensor(out=ld[:, j % 2], in0=tx[:, j % 2, 0:256], scalar=0.0, in1=lt[:, j % 2],
                                             op0=ALU.min, op1=ALU.subtract).then_inc(s_txf, 1)
                items = slots(nt)
                for n in range(len(items) + 1):
                    if n >= 1:
                        g, j = items[n - 1]
                        if g <= K_:
                            q = g * nt + j
                            c = b * 2 * BT + q
                            dve.wait_ge(s_qq, c + 1)
                            dve.tensor_tensor(nq[:, q % 2].rearrange("p (h d) -> p h d", d=HD),
                                              pj[:, (n - 1) % 4].rearrange("p (h d) -> p h d", d=HD),
                                              r8[:, q % 2].unsqueeze(2).to_broadcast([P, SB_HEADS, HD]), ALU.mult).then_inc(s_bank, 1)
                    if n < len(items):
                        g, j = items[n]
                        bank = pj[:, n % 4]
                        if g <= K_:
                            q = g * nt + j
                            dve.wait_ge(s_qs, b * 2 * BT + q + 1)
                            dve.tensor_reduce(ss8[:, q % 2], tmp[:, q % 2].rearrange("p (h d) -> p h d", d=HD),
                                              AX.X, ALU.add).then_inc(s_qr, 1)
                        elif g == V_:
                            dve.wait_ge(s_vh, b * BT + j + 1)
                            dve.tensor_tensor(vst[:, j % 2, :, 1, :], bank.rearrange("p (h d) -> p h d", d=HD),
                                              raw(vst[:, j % 2, :, 0, :]), ALU.subtract).then_inc(s_bank, 1)
                        else:
                            q = (g - 3) * nt + j
                            dve.wait_ge(s_ngd[q % 2], 16 * (b * 3 * BT // 2 + q // 2))
                            if g == GATE_:
                                dve.wait_ge(s_gp, b * BT + j + 1)
                                dve.reciprocal(ge[:, j % 2], ge[:, j % 2]).then_inc(s_gr, 1)
                                dve.wait_ge(s_gr, b * BT + j + 1)
                                dve.tensor_tensor(ng[:, q % 2], bank, ge[:, j % 2], ALU.mult).then_inc(s_bank, 1)
                            else:
                                dve.wait_ge(s_pj, b * NG * BT + n + 1 + BT)
                                dve.tensor_copy(ng[:, q % 2], bank).then_inc(s_bank, 1)
                    if n >= 1:
                        g, j = items[n - 1]
                        if g <= K_:
                            q = g * nt + j
                            dve.wait_ge(s_qh, b * 2 * BT + q + 1)
                            src = kn[:, j % 2] if g == K_ else nq[:, q % 2]
                            dve.tensor_tensor(stk[:, q % 2, :, 1, :], src.rearrange("p (h d) -> p h d", d=HD),
                                              raw(stk[:, q % 2, :, 0, :]), ALU.subtract).then_inc(s_ql, 1)

            blocks_loop(dve, body)

        @block.tensor
        def _(pe):
            pe.sem_inc(s_pj, BT)
            pe.sem_inc(s_tT, RING)
            pe.wait_ge(s_c, 96)
            pe.wait_ge(s_cs, 3)
            pe.wait_ge(s_wal, 1)

            def body(b, nt, last):
                for j in range(nt):
                    pe.wait_ge(s_xn, b * BT + j + 1 + RING)
                    for a in range(2):
                        pe.wait_ge(s_txf, b * TX_USES + 2 * j + a + 1)
                        for c in range(4):
                            k = 4 * a + c
                            mm = pe.transpose(tx[:, a, c * P:(c + 1) * P], xn[:, j % 2, k * P:(k + 1) * P], idt[:])
                        mm.then_inc(s_tx, 1)
                half = nt * P // 2
                for a in range(2):
                    if a == 0:
                        pe.wait_ge(s_txf, b * TX_USES + 2 * nt + RING)
                    for i, (w, xx) in enumerate(((wah, xh), (wah, xl), (wal, xh))):
                        for k in range(KC):
                            mm = pe.matmul(tx[:, a, 0:half], w[:, k, :], xx[:, k, a * half:(a + 1) * half],
                                           start=(i == 0 and k == 0), stop=(i == 2 and k == KC - 1))
                    mm.then_inc(s_tx, 1)
                for j in range(nt):
                    pe.wait_ge(s_txf, b * TX_USES + 2 * nt + RING + max(2, 1 + j))
                    pe.matmul(tx[:, j % 2, 0:256], alrT[0:RANK + 1, j * P:(j + 1) * P], wa2[0:RANK + 1, :],
                              start=True, stop=True).then_inc(s_tx, 1)
                items = slots(nt)
                for n in range(len(items) + 2):
                    if n < len(items):
                        g, j = items[n]
                        if j == 0:
                            pe.wait_ge(s_wl, b * NG + g + 1)
                        pe.wait_ge(s_bank, b * NG * BT + n + 1)
                        ts = slice(j * P, (j + 1) * P)
                        for i, (xx, w) in enumerate(((xh, wh), (xh, wl), (xl, wh))):
                            for k in range(KC):
                                mm = pe.matmul(pj[:, n % 4], xx[:, k, ts], w[:, g % 2, k, :],
                                               start=(i == 0 and k == 0), stop=(i == 2 and k == KC - 1))
                        mm.then_inc(s_pj, 1)
                    if n >= 2:
                        g, j = items[n - 2]
                        if g <= K_:
                            q = g * nt + j
                            c = b * 2 * BT + q
                            pe.wait_ge(s_ql, c + 1)
                            for a in range(2):
                                pe.wait_ge(s_ev, 2 * c + a + 1)
                                for h in range(4):
                                    mm = pe.transpose(tT[:, a, h * P:(h + 1) * P],
                                                      raw(stk[:, q % 2, 4 * a + h]).rearrange("p a d -> p (a d)"), idt[:])
                                mm.then_inc(s_tT, 1)

            blocks_loop(pe, body)


NL = len(LEVELS)
DCOLS = (NL + 1) * P
SCOLS = NL * CHUNK + P


def right(ap, level):
    return ap.rearrange("p (n a l) -> p n a l", a=2, l=LEVELS[level])[:, :, 1, :]


def phase_gla(nc, gqk, gv, sgate, la, gla_g, state_in, ident, sum_mats, end_mat, score_mask, mix, new_state):
    with Pool(nc, "gl") as m:
        idt = m.sb("idt", [P, P])
        am = m.sb("am", [P, DCOLS])
        ae = m.sb("ae", [P, P])
        mask = m.sb("mask", [P, SCOLS])
        gb = m.sb("gb", [P, GLA_HEADS, DV])
        half_pow = m.sb("half_pow", [P, GLA_HEADS])
        qk = m.sb("qk", [P, 2, 512])
        lat = m.sb("lat", [P, 2, 256])
        sg = m.sb("sg", [P, 2, 512])
        v = m.sb("v", [P, 2, 512])
        qkT = m.sb("qkT", [P, 2, 4, P])
        ex = m.sb("ex", [P, 2, 2, DCOLS])
        kx = m.sb("kx", [P, 2, 2, NL, P])
        qx = m.sb("qx", [P, 2, 2, NL, P])
        qb = m.sb("qb", [P, 2, 2, 3 * P])
        ken = m.sb("ken", [P, 2, 256])
        ke = m.sb("ke", [P, 2, 256])
        sm = m.sb("sm", [P, 2, SCOLS])
        st = m.sb("st", [P, 2, 2, 2, DV])
        o2 = m.sb("o2", [P, 512])
        ss4 = m.sb("ss4", [P, GLA_HEADS])
        ms4 = m.sb("ms4", [P, GLA_HEADS])
        r4 = m.sb("r4", [P, GLA_HEADS])
        on = m.sb("on", [P, 512])
        sgg = m.sb("sgg", [P, 3, 512])
        mo = m.sb("mo", [P, 2, 512])
        pt = m.ps("pt", [P, 512])
        pd = m.ps("pd", [P, 2, 512])
        pn = m.ps("pn", [P, 512])
        psc = m.ps("psc", [P, 2, 512])
        po = m.ps("po", [P, 512])
        pu = m.ps("pu", [P, 512])
        names = ("c", "cs", "tr", "trq", "trk", "d", "dx", "kx", "qx", "qb", "n", "nx", "ke", "sgg",
                 "ua", "st", "sc", "sm", "as", "o", "sq", "ss", "ms", "r", "on", "mo")
        (s_c, s_cs, s_tr, s_trq, s_trk, s_d, s_dx, s_kx, s_qx, s_qb, s_n, s_nx, s_ke, s_sgg,
         s_ua, s_st, s_sc, s_sm, s_as, s_o, s_sq, s_ss, s_ms, s_r, s_on, s_mo) = [m.sem(n) for n in names]
        s_in, s_v, s_md = m.sems("in", 2), m.sems("v", 2), m.sems("md", 2)
        s_pass_sp, s_pass_pe, s_pass_pool = m.sem("pass_sp"), m.sem("pass_pe"), m.sem("pass_pool")
        s_si, s_so, s_sp = m.sem("si"), m.sem("so"), m.sem("sp")
        block = m.block()
        LAST = TILES - 1

        def pipeline(eng, slot):
            slot(0, 0, (1,), False)
            slot(0, 1, (1, 2), False)
            with eng.Fori(0, (LAST - 2) // 2) as i:
                slot(i + 1, 0, (3, 1, 2), False)
                slot(i + 1, 1, (3, 1, 2), False)
            slot(LAST // 2, 0, (3, 1, 2), False)
            slot(LAST // 2, 1, (3, 2), True)
            slot(LAST // 2 + 1, 0, (3,), False)

        def before(h, p, n):
            q = p - n
            h = h + q // 2
            return h, q % 2, h * 2 + q % 2

        @block.sync
        def _(sp):
            sp.dma_start(idt[:], ident).then_inc(s_c, 16)
            sp.dma_start(am[:], sum_mats).then_inc(s_c, 16)
            sp.dma_start(ae[:], end_mat).then_inc(s_c, 16)
            sp.dma_start(mask[:], score_mask).then_inc(s_c, 16)
            for h in range(GLA_HEADS):
                sp.dma_start(gb[:, h], bcast_rows(gla_g, DV)).then_inc(s_c, 16)

            def load(h, p):
                t = h * 2 + p
                for dst, src in ((qk, gqk), (lat, la), (sg, sgate)):
                    sp.dma_start(dst[:, p], rows(src, t)).then_inc(s_in[p], 16)

            load(0, 0)
            load(0, 1)

            def slot(h, p, stages, sample):
                t = h * 2 + p
                if 1 in stages:
                    if 3 in stages:
                        sp.wait_ge(s_o, 4 * (t - 1))
                    sp.dma_start(v[:, p], rows(gv, t)).then_inc(s_v[p], 16)
                if 3 in stages:
                    h2, p2, t2 = before(h, p, 2)
                    sp.wait_ge(s_mo, t2 + 1)
                    sp.dma_start(mix[bass.ds(t2 * P, P), 0:512], mo[:, p2]).then_inc(s_md[p2], 16)
                if sample:
                    sp.wait_ge(s_st, 4 * LAST)
                    ns = st[:, LAST % 2, 0]
                    sp.dma_start(new_state[0].rearrange("(a b) k v -> (b k) a v", b=2), ns).then_inc(s_so, 16)
                    sp.wait_ge(s_so, 16)
                    sp.dma_start(ns, state_in.rearrange("(a b) k v -> (b k) a v", b=2)).then_inc(s_si, 16)
                if 1 in stages and 2 in stages and not (isinstance(h, int) and h * 2 + p >= LAST):
                    sp.wait_ge(s_qb, 2 * t)
                    sp.wait_ge(s_ke, t)
                    stop_at(sp, s_sgg, t, s_pass_sp)
                    h1, p1, t1 = before(h, p, -1)
                    load(h1, p1)

            pipeline(sp, slot)
            sp.wait_ge(s_st, 4 * LAST + 2)
            sp.dma_start(new_state[1].rearrange("(a b) k v -> (b k) a v", b=2), st[:, LAST % 2, 1]).then_inc(s_so, 16)
            sp.wait_ge(s_so, 32)
            sp.wait_ge(s_md[0], 16 * (TILES // 2 + 1))
            sp.wait_ge(s_md[1], 16 * (TILES // 2))

        @block.tensor
        def _(pe):
            pe.wait_ge(s_c, 128)

            def stage1(h, p):
                t = h * 2 + p
                pe.wait_ge(s_in[p], 48 * (h + 1))
                pe.wait_ge(s_trq, t)
                pe.wait_ge(s_trk, t)
                for c in range(4):
                    mm = pe.transpose(pt[:, c * P:(c + 1) * P], qk[:, p, c * P:(c + 1) * P], idt[:])
                mm.then_inc(s_tr, 1)
                for a in range(2):
                    for i, (lo, hi) in enumerate(((0, 512), (512, DCOLS))):
                        pe.wait_ge(s_dx, 4 * t + 2 * a + i - 1 if a or i else 4 * t)
                        pe.matmul(pd[:, i, 0:hi - lo], lat[:, p, a * P:(a + 1) * P], am[:, lo:hi],
                                  start=True, stop=True).then_inc(s_d, 1)
                pe.wait_ge(s_nx, t)
                pe.matmul(pn[:, 0:256], ae[:], lat[:, p, :], start=True, stop=True).then_inc(s_n, 1)

            def chunk_update(p, c):
                for hd in range(GLA_HEADS):
                    a, half = hd // 2, slice(64 * (hd % 2), 64 * (hd % 2) + 64)
                    tok = slice(CHUNK * c, CHUNK * c + CHUNK)
                    mm = pe.matmul(pu[half, a * DV:(a + 1) * DV], ke[tok, p, hd * DK:(hd + 1) * DK],
                                   v[tok, p, hd * DV:(hd + 1) * DV], start=True, stop=True)
                mm.then_inc(s_ua, 1)

            def scores(h, p, t, hd):
                a, half = hd // 2, slice(64 * (hd % 2), 64 * (hd % 2) + 64)
                pe.wait_ge(s_sm, 4 * t + max(hd - 1, 0))
                for i in range(NL):
                    pe.matmul(psc[:, hd % 2, i * CHUNK:(i + 1) * CHUNK], kx[half, p, a, i, :], right(qx[half, p, a, i, :], i),
                              start=True, stop=True)
                pe.matmul(psc[:, hd % 2, NL * CHUNK:SCOLS], qkT[half, p, 2 + a, :], qkT[half, p, a, :],
                          start=True, stop=True).then_inc(s_sc, 1)

            def outputs(h, p, t, hd):
                a, half = hd // 2, slice(64 * (hd % 2), 64 * (hd % 2) + 64)
                dst = po[:, hd * DV:(hd + 1) * DV]
                pe.wait_ge(s_as, 4 * t + hd + 1)
                pe.wait_ge(s_o, 4 * t + hd)
                pe.matmul(dst, sm[:, hd % 2, NL * CHUNK:SCOLS], v[:, p, hd * DV:(hd + 1) * DV], start=True, stop=False)
                pe.matmul(dst, qb[half, p, a, 0:P], st[half, p, 0, a], start=False, stop=False)
                pe.matmul(dst, qb[half, p, a, P:2 * P], st[half, p, 1, a], start=False, stop=True).then_inc(s_o, 1)

            def slot(h, p, stages, sample):
                if 1 in stages:
                    stage1(h, p)
                if 2 in stages:
                    h1, p1, t = before(h, p, 1)
                    pe.wait_ge(s_v[p1], 16 * (h1 + 1))
                    pe.wait_ge(s_ke, t + 1)
                    stop_at(pe, s_st, 4 * t, s_pass_pe)
                    chunk_update(p1, 0)
                    pe.wait_ge(s_kx, 2 * t + 2)
                    pe.wait_ge(s_qx, 2 * t + 2)
                    scores(h1, p1, t, 0)
                    scores(h1, p1, t, 1)
                    stop_at(pe, s_st, 4 * t + 2, s_pass_pe)
                    chunk_update(p1, 1)
                    pe.wait_ge(s_on, t)
                    pe.wait_ge(s_qb, 2 * t + 2)
                    if sample:
                        pe.wait_ge(s_si, 16)
                    outputs(h1, p1, t, 0)
                    scores(h1, p1, t, 2)
                    outputs(h1, p1, t, 1)
                    scores(h1, p1, t, 3)
                    outputs(h1, p1, t, 2)
                    outputs(h1, p1, t, 3)

            pipeline(pe, slot)

        @block.scalar
        def _(act):
            act.preload_act_table_set("natural_log_exp_and_others")

            def slot(h, p, stages, sample):
                if 3 in stages:
                    h2, p2, t2 = before(h, p, 2)
                    act.wait_ge(s_o, 4 * (t2 + 1))
                    act.wait_ge(s_ss, t2)
                    act.activation(o2[:], po[:], ACT.Square).then_inc(s_sq, 1)
                if 1 in stages:
                    t = h * 2 + p
                    act.wait_ge(s_tr, t + 1)
                    if 3 in stages:
                        act.wait_ge(s_o, 4 * (t - 1))
                    act.activation(qkT[:, p, 0:2], pt[:, 0:2 * P].rearrange("p (c k) -> p c k", k=P), ACT.Copy,
                                   scale=DK ** -0.5).then_inc(s_trq, 1)
                    for a in range(2):
                        for i, (lo, hi) in enumerate(((0, 512), (512, DCOLS))):
                            act.wait_ge(s_d, 4 * t + 2 * a + i + 1)
                            act.activation(ex[:, p, a, lo:hi], pd[:, i, 0:hi - lo], ACT.Exp, scale=1.0 / GATE_NORM).then_inc(s_dx, 1)
                    act.wait_ge(s_n, t + 1)
                    act.activation(ken[:, p], pn[:, 0:256], ACT.Exp, scale=1.0 / GATE_NORM).then_inc(s_nx, 1)

            pipeline(act, slot)

        @block.vector
        def _(dve):
            dve.memset(st[:, 0, 0], 0.0).then_inc(s_sp, 1)
            dve.memset(qb[:], 0.0).then_inc(s_sp, 1)
            dve.wait_ge(s_sp, 2)
            dve.wait_ge(s_c, 128)

            def new_states(h, p, t, c, sample):
                dve.wait_ge(s_ua, 2 * t + c + 1)
                for a in range(2):
                    src = st[:, p, c, a]
                    dst = st[:, p, 1, a] if c == 0 else st[:, 1 - p, 0, a]
                    end = NL * P + CHUNK * c + CHUNK - 1
                    dve.scalar_tensor_tensor(out=dst, in0=src, scalar=ex[:, p, a, end:end + 1], in1=pu[:, a * DV:(a + 1) * DV],
                                             op0=ALU.mult, op1=ALU.add).then_inc(s_st, 1)

            def masked(t, hd):
                dve.wait_ge(s_sc, 4 * t + hd + 1)
                if hd >= 2 or not isinstance(t, int) or t > 0:
                    dve.wait_ge(s_o, 4 * t + hd - 1)
                dve.tensor_tensor(sm[:, hd % 2], psc[:, hd % 2], mask[:], ALU.mult).then_inc(s_sm, 1)

            def slot(h, p, stages, sample):
                if 3 in stages:
                    h2, p2, t2 = before(h, p, 2)
                    dve.wait_ge(s_sq, t2 + 1)
                    dve.tensor_reduce(ss4[:], o2[:].rearrange("p (h d) -> p h d", d=DV), AX.X, ALU.add).then_inc(s_ss, 1)
                if 1 in stages:
                    t = h * 2 + p
                    dve.wait_ge(s_tr, t + 1)
                    dve.wait_ge(s_trq, t + 1)
                    dve.tensor_copy(qkT[:, p, 2:4], pt[:, 2 * P:4 * P].rearrange("p (c k) -> p c k", k=P)).then_inc(s_trk, 1)
                    dve.wait_ge(s_trk, t + 1)
                    for a in range(2):
                        dve.wait_ge(s_dx, 4 * t + 2 * a + 2)
                        dve.tensor_tensor(kx[:, p, a], ex[:, p, a, 0:NL * P].rearrange("p (l k) -> p l k", k=P),
                                          qkT[:, p, 2 + a:3 + a].to_broadcast([P, NL, P]), ALU.mult).then_inc(s_kx, 1)
                        dve.tensor_tensor(qb[:, p, a].rearrange("p (c x) -> p c x", x=3 * CHUNK)[:, :, 0:CHUNK],
                                          ex[:, p, a, NL * P:DCOLS].rearrange("p (c x) -> p c x", x=CHUNK),
                                          qkT[:, p, a].rearrange("p (c x) -> p c x", x=CHUNK), ALU.mult).then_inc(s_qb, 1)
                    dve.wait_ge(s_nx, t + 1)
                    dve.wait_ge(s_in[p], 48 * (h + 1))
                    dve.tensor_tensor(ke[:, p], qk[:, p, 256:512], ken[:, p], ALU.mult).then_inc(s_ke, 1)
                if 3 in stages:
                    dve.wait_ge(s_r, t2 + 1)
                    dve.wait_ge(s_mo, t2)
                    dve.tensor_tensor(on[:].rearrange("p (h d) -> p h d", d=DV), po[:].rearrange("p (h d) -> p h d", d=DV),
                                      r4[:].unsqueeze(2).to_broadcast([P, GLA_HEADS, DV]), ALU.mult).then_inc(s_on, 1)
                if 2 in stages:
                    h1, p1, t = before(h, p, 1)
                    if sample:
                        dve.wait_ge(s_si, 16)
                    new_states(h1, p1, t, 0, sample)
                    masked(t, 0)
                    masked(t, 1)
                    dve.wait_ge(s_st, 4 * t + 2)
                    new_states(h1, p1, t, 1, sample)
                    masked(t, 2)
                    masked(t, 3)

            pipeline(dve, slot)

        @block.gpsimd
        def _(pool):
            pool.memset(half_pow[:], -0.5).then_inc(s_cs, 1)
            pool.wait_ge(s_cs, 1)
            pool.wait_ge(s_c, 128)

            def slot(h, p, stages, sample):
                if 3 in stages:
                    h2, p2, t2 = before(h, p, 2)
                    stop_at(pool, s_ss, t2 + 1, s_pass_pool)
                    pool.tensor_scalar(ms4[:], ss4[:], 1.0 / DV, EPS, ALU.mult, ALU.add).then_inc(s_ms, 1)
                    pool.wait_ge(s_ms, t2 + 1)
                    pool.wait_ge(s_on, t2)
                    pool.tensor_tensor(r4[:], ms4[:], half_pow[:], ALU.pow).then_inc(s_r, 1)
                if 1 in stages:
                    t = h * 2 + p
                    for a in range(2):
                        pool.wait_ge(s_trq, t + 1)
                        pool.wait_ge(s_dx, 4 * t + 2 * a + 2)
                        pool.tensor_tensor(qx[:, p, a], ex[:, p, a, 0:NL * P].rearrange("p (l k) -> p l k", k=P),
                                           qkT[:, p, a:a + 1].to_broadcast([P, NL, P]), ALU.mult).then_inc(s_qx, 1)
                if 3 in stages:
                    pool.wait_ge(s_on, t2 + 1)
                    pool.wait_ge(s_md[p2], 16 * h2)
                    pool.tensor_tensor(mo[:, p2], on[:], sgg[:, p2], ALU.mult).then_inc(s_mo, 1)
                if 2 in stages:
                    h1, p1, t = before(h, p, 1)
                    pool.wait_ge(s_in[p1], 48 * (h1 + 1))
                    if 3 in stages:
                        pool.wait_ge(s_mo, t - 1)
                    pool.tensor_tensor(sgg[:, p1], sg[:, p1], gb[:].rearrange("p h d -> p (h d)"), ALU.mult).then_inc(s_sgg, 1)
                    for hd in range(GLA_HEADS):
                        pool.wait_ge(s_sm, 4 * t + hd + 1)
                        whole = sm[:, hd % 2, NL * CHUNK:SCOLS]
                        for i in range(NL):
                            part = sm[:, hd % 2, i * CHUNK:(i + 1) * CHUNK].rearrange("p (n l) -> p n l", l=LEVELS[i])
                            last = pool.tensor_tensor(right(whole, i), right(whole, i), part, ALU.add)
                            if i < NL - 1:
                                last.then_inc(s_cs, 1)
                                pool.wait_ge(s_cs, t * (4 * (NL - 1)) + hd * (NL - 1) + i + 2)
                        last.then_inc(s_as, 1)

            pipeline(pool, slot)


def attention_units():
    units = []
    for t in range(TILES):
        lo, n = (0, t + 1) if t < TILES - 1 else (SEQ // P, PAST // P + 1)
        if n <= 8:
            units.append((t, lo, n, True, True))
        else:
            low = n // 2
            units.append((t, lo + low, n - low, True, False))
            units.append((t, lo, low, False, True))
    return units


def phase_attention(nc, qT, kT, vS, ident, diag_mask, mix):
    units = [(p, *u) for p in range(2) for u in attention_units()]
    NU = len(units)
    groups = [[(u, g, min(4, n - 4 * g)) for g in range((n + 3) // 4)] for u, (_, _, _, n, _, _) in enumerate(units)]
    first_group = [sum(len(g) for g in groups[:u]) for u in range(NU + 1)]
    NGR = first_group[NU]
    tiles_done = [sum(x[5] for x in units[:u]) for u in range(NU + 1)]
    NT = 2 * TILES
    on_act = [gi % 2 == 1 for gi in range(NGR)]
    act_before = [sum(on_act[:gi]) for gi in range(NGR + 1)]
    with Pool(nc, "sb") as m:
        idt = m.sb("idt", [P, P])
        idr = m.sb("idr", [P, P], F32R)
        dm = m.sb("dm", [P, P])
        dmr = m.sb("dmr", [P, P], F32R)
        kt = m.sb("kt", [P, 2, KEYS], F32R)
        qh = m.sb("qh", [P, 2, ROWS], F32R)
        ql = m.sb("ql", [P, 2, ROWS], F32R)
        v = m.sb("v", [P, 2, KEYS // P, P], F32R)
        a = m.sb("a", [P, 3, 1024])
        g = m.sb("g", [P, 2, 1024])
        w = m.sb("w", [P, 2, 1024])
        ssum = m.sb("ssum", [P, 1])
        wth = m.sb("wth", [P, 4, 512], F32R)
        wtl = m.sb("wtl", [P, 4, 512], F32R)
        os_ = m.sb("os", [P, 2, TILES, HD])
        z = m.ps("z", [P, 2, 1024])
        tp = m.ps("tp", [P, 2, 512])
        po = m.ps("po", [P, 2, 512])
        names = ("c", "cr", "z", "ab", "ex", "ln", "sp", "ss", "gt", "sc", "w", "tr", "wh", "wl", "pv", "of", "wha")
        s_c, s_cr, s_z, s_ab, s_ex, s_ln, s_sp, s_ss, s_gt, s_sc, s_w, s_tr, s_wh, s_wl, s_pv, s_of, s_wha = [m.sem(n) for n in names]
        s_in, s_os = m.sems("in", 2), m.sems("os", 2)
        block = m.block()

        def ago(i, u, n, per):
            return i * per + max(u - n + 1, 0)

        def head(ap, h):
            return ap[bass.ds(h, 1)].rearrange("o p k -> p (o k)")

        @block.sync
        def _(sp):
            sp.dma_start(idt[:], ident).then_inc(s_c, 16)
            sp.dma_start(dm[:], diag_mask).then_inc(s_c, 16)

            def load(h, p):
                sp.dma_start(raw(kt[:, p]), head(kT, h)).then_inc(s_in[p], 16)
                for half in range(2):
                    ps = slice(64 * half, 64 * half + 64)
                    sp.dma_start(raw(qh[ps, p]), head(qT, h)[0:64]).then_inc(s_in[p], 16)
                    sp.dma_start(raw(ql[ps, p]), head(qT, h)[64:128]).then_inc(s_in[p], 16)
                sp.dma_start(raw(v[:, p]), vS[:, bass.ds(h * P, P)].rearrange("(t p) c -> p t c", p=P)).then_inc(s_in[p], 16)

            def turn(i, last):
                for p in range(2):
                    if p == 0 or not last:
                        sp.wait_ge(s_pv, i * NGR + first_group[p * NU // 2])
                        load(2 * i + 1 + p, 1 - p)
                    sp.wait_ge(s_of, i * NT + (p + 1) * TILES)
                    sp.dma_start(mix[:, bass.ds((2 * i + p) * HD + 512, HD)].rearrange("(t p) c -> p t c", p=P),
                                 os_[:, p]).then_inc(s_os[p], 16)

            load(0, 0)
            with sp.Fori(0, SB_HEADS // 2 - 1) as i:
                turn(i, False)
            turn(SB_HEADS // 2 - 1, True)
            for p in range(2):
                sp.wait_ge(s_os[p], 16 * SB_HEADS // 2)

        @block.tensor
        def _(pe):
            pe.wait_ge(s_cr, 2)

            def logits(i, u):
                p, t, lo, n, first, last = units[u]
                if u % (NU // 2) == 0:
                    pe.wait_ge(s_in[p], 96 * (i + 1))
                pe.wait_ge(s_sc, ago(i, u, 2, NU))
                for b in range((n + 3) // 4):
                    nb = min(4, n - 4 * b)
                    dst = z[:, u % 2, 512 * b:512 * b + nb * P]
                    keys = kt[:, p, (lo + 4 * b) * P:(lo + 4 * b + nb) * P]
                    masked = first and 4 * b + nb == n
                    pe.matmul(dst, qh[:, p, t * P:(t + 1) * P], keys, start=True, stop=False)
                    mm = pe.matmul(dst, ql[:, p, t * P:(t + 1) * P], keys, start=False, stop=not masked)
                    if masked:
                        mm = pe.matmul(z[:, u % 2, (n - 1) * P:n * P], idr[:], dmr[:], start=False, stop=True)
                mm.then_inc(s_z, 1)

            def transposes(i, u):
                pe.wait_ge(s_w, i * NU + u + 1)
                for j, (_, g4, nb) in enumerate(groups[u]):
                    gi = first_group[u] + j
                    pe.wait_ge(s_wl, i * NGR + max(gi - 1, 0))
                    for c in range(nb):
                        mm = pe.transpose(tp[:, gi % 2, c * P:(c + 1) * P], w[:, u % 2, (4 * g4 + c) * P:(4 * g4 + c + 1) * P], idt[:])
                    mm.then_inc(s_tr, 1)

            def values(i, u):
                p, t, lo, n, first, last = units[u]
                tt = tiles_done[u]
                if first:
                    pe.wait_ge(s_of, i * NT + max(tt - 1, 0))
                for j, (_, g4, nb) in enumerate(groups[u]):
                    gi = first_group[u] + j
                    pe.wait_ge(s_wl, i * NGR + gi + 1)
                    for c in range(nb):
                        key = lo + 4 * g4 + c
                        for part in (wth, wtl):
                            mm = pe.matmul(po[:, tt % 2, 0:P], part[:, gi % 4, c * P:(c + 1) * P], v[:, p, key],
                                           start=(first and j == 0 and c == 0 and part is wth),
                                           stop=(last and 4 * g4 + c == n - 1 and part is wtl))
                    mm.then_inc(s_pv, 1)

            with pe.Fori(0, SB_HEADS // 2) as i:
                logits(i, 0)
                for s in range(NU + 3):
                    if 0 <= s - 2 < NU:
                        transposes(i, s - 2)
                    if s + 1 < NU:
                        logits(i, s + 1)
                    if 0 <= s - 3 < NU:
                        values(i, s - 3)

        @block.scalar
        def _(act):
            act.preload_act_table_set("natural_log_exp_and_others")
            act.wait_ge(s_c, 32)
            act.activation(idr[:], idt[:], ACT.Copy).then_inc(s_cr, 1)
            act.activation(dmr[:], dm[:], ACT.Copy).then_inc(s_cr, 1)

            def absolute(i, u):
                act.wait_ge(s_z, i * NU + u + 1)
                act.wait_ge(s_sc, ago(i, u, 3, NU))
                n = units[u][3] * P
                act.activation(a[:, u % 3, 0:n], z[:, u % 2, 0:n], ACT.Abs).then_inc(s_ab, 1)

            def weights(i, u):
                act.wait_ge(s_sc, i * NU + u + 1)
                act.wait_ge(s_tr, i * NGR + first_group[max(u - 1, 0)])
                n = units[u][3] * P
                act.activation(w[:, u % 2, 0:n], g[:, u % 2, 0:n], ACT.Exp, scale=-1.0).then_inc(s_w, 1)

            def high_halves(i, u):
                for j, (_, g4, nb) in enumerate(groups[u]):
                    gi = first_group[u] + j
                    if on_act[gi]:
                        act.wait_ge(s_tr, i * NGR + gi + 1)
                        act.wait_ge(s_pv, i * NGR + max(gi - 3, 0))
                        act.activation(wth[:, gi % 4, 0:nb * P], tp[:, gi % 2, 0:nb * P], ACT.Copy).then_inc(s_wha, 1)

            with act.Fori(0, SB_HEADS // 2) as i:
                absolute(i, 0)
                for s in range(NU + 3):
                    n = units[s][3] * P if s < NU else 0
                    if s < NU:
                        act.wait_ge(s_ab, i * NU + s + 1)
                        act.activation(a[:, s % 3, 0:n], a[:, s % 3, 0:n], ACT.Exp, scale=-1.0).then_inc(s_ex, 1)
                    if s < NU:
                        act.wait_ge(s_ex, i * NU + s + 1)
                        act.activation(a[:, s % 3, 0:n], a[:, s % 3, 0:n], ACT.Ln, bias=1.0).then_inc(s_ln, 1)
                    if 0 <= s - 2 < NU:
                        high_halves(i, s - 2)
                    if 0 <= s - 1 < NU:
                        weights(i, s - 1)
                    if s + 1 < NU:
                        absolute(i, s + 1)

        @block.vector
        def _(dve):
            followed = [not x[5] for x in units]
            nf = [sum(followed[:u]) for u in range(NU + 1)]

            def negated_softplus(i, u):
                n = units[u][3] * P
                dve.wait_ge(s_ln, i * NU + u + 1)
                dve.scalar_tensor_tensor(out=a[:, u % 3, 0:n], in0=z[:, u % 2, 0:n], scalar=0.0, in1=a[:, u % 3, 0:n],
                                         op0=ALU.min, op1=ALU.subtract).then_inc(s_sp, 1)
                dve.wait_ge(s_w, ago(i, u, 2, NU))
                top = g[:, u % 2, n - 1:n]
                if units[u][4]:
                    dve.memset(top, -NEG).then_inc(s_gt, 1)
                else:
                    dve.wait_ge(s_sp, i * NU + u + 1)
                    dve.wait_ge(s_sc, i * NU + u)
                    dve.tensor_tensor(top, ssum[:], a[:, u % 3, n - 1:n], ALU.subtract).then_inc(s_gt, 1)

            def scan(i, u):
                n = units[u][3] * P
                dve.wait_ge(s_sp, i * NU + u + 1)
                dve.wait_ge(s_gt, i * NU + u + 1)
                ins = dve.tensor_tensor_scan(g[:, u % 2, n - 2::-1], z[:, u % 2, n - 1:0:-1], a[:, u % 3, n - 2::-1],
                                             g[:, u % 2, n - 1:n], ALU.add, ALU.subtract)
                if followed[u]:
                    ins.then_inc(s_ss, 1)
                    dve.wait_ge(s_ss, i * nf[NU] + nf[u] + 1)
                    ins = dve.tensor_tensor(ssum[:], g[:, u % 2, 0:1], z[:, u % 2, 0:1], ALU.add)
                ins.then_inc(s_sc, 1)

            def halves(i, u):
                for j, (_, g4, nb) in enumerate(groups[u]):
                    gi = first_group[u] + j
                    c = nb * P
                    if on_act[gi]:
                        dve.wait_ge(s_wha, i * act_before[NGR] + act_before[gi] + 1)
                    else:
                        dve.wait_ge(s_tr, i * NGR + gi + 1)
                        dve.wait_ge(s_pv, i * NGR + max(gi - 3, 0))
                        dve.tensor_copy(wth[:, gi % 4, 0:c], tp[:, gi % 2, 0:c]).then_inc(s_wh, 1)
                        dve.wait_ge(s_wh, i * (NGR - act_before[NGR]) + gi - act_before[gi] + 1)
                    dve.tensor_tensor(wtl[:, gi % 4, 0:c], tp[:, gi % 2, 0:c], raw(wth[:, gi % 4, 0:c]), ALU.subtract).then_inc(s_wl, 1)

            def output(i, u):
                p, t, lo, n, first, last = units[u]
                if last:
                    tt = tiles_done[u]
                    dve.wait_ge(s_pv, i * NGR + first_group[u + 1])
                    if t == 0:
                        dve.wait_ge(s_os[p], 16 * i)
                    dve.tensor_reduce(os_[:, p, t, :], po[:, tt % 2, 0:P].rearrange("p (a d) -> p d a", a=2), AX.X, ALU.add).then_inc(s_of, 1)

            with dve.Fori(0, SB_HEADS // 2) as i:
                for s in range(NU + 4):
                    if 0 <= s - 4 < NU:
                        output(i, s - 4)
                    if s < NU:
                        negated_softplus(i, s)
                    if 0 <= s - 2 < NU:
                        halves(i, s - 2)
                    if s < NU:
                        scan(i, s)


def phase_output(nc, mix, x, w_out, norm_g, ident, h_out, hTh, hTl):
    with Pool(nc, "ot") as m:
        idt = m.sb("idt", [P, P])
        gb = m.sb("gb", [P, D])
        half_pow = m.sb("half_pow", [P, 1])
        wr = m.sb("wr", [P, 2, KC, 512])
        wh = m.sb("wh", [P, 2, KC, 512], F32R)
        wl = m.sb("wl", [P, 2, KC, 512], F32R)
        mi = m.sb("mi", [P, 2, D])
        xb = m.sb("xb", [P, 2, D])
        mh = m.sb("mh", [P, 2, KC, P], F32R)
        ml = m.sb("ml", [P, 2, KC, P], F32R)
        hb = m.sb("hb", [P, 2, D])
        hn = m.sb("hn", [P, 2, D])
        ss = m.sb("ss", [P, 2, 3])
        sh = m.sb("sh", [P, 2, KC, P], F32R)
        sl = m.sb("sl", [P, 2, KC, P], F32R)
        ta = m.ps("ta", [P, D])
        tb = m.ps("tb", [P, D])
        pp = m.ps("pp", [P, 2, D])
        names = ("c", "cs", "wh", "wl0", "wl1", "a", "mh", "ml", "b", "h", "sq", "ms", "r", "hn", "t", "sh", "sl")
        s_c, s_cs, s_wh, s_wl0, s_wl1, s_a, s_mh, s_ml, s_b, s_h, s_sq, s_ms, s_r, s_hn, s_t, s_sh, s_sl = [m.sem(n) for n in names]
        s_w = m.sems("w", 2)
        s_pass_sp, s_pass_pool = m.sem("pass_sp"), m.sem("pass_pool")
        s_m, s_x, s_ho, s_ho2 = m.sems("m", 2), m.sems("x", 2), m.sems("ho", 2), m.sems("ho2", 2)
        block = m.block()

        def pipeline(eng, slot):
            slot(0, 0, "A")
            slot(0, 1, "AB")
            with eng.Fori(0, (TILES - 3) // 2) as i:
                slot(i + 1, 0, "ABC")
                slot(i + 1, 1, "ABC")
            slot((TILES - 1) // 2, 0, "ABC")
            slot((TILES - 1) // 2, 1, "BC")
            slot((TILES + 1) // 2, 0, "C")

        def before(k, p, n):
            q = p - n
            k = k + q // 2
            return k, q % 2, k * 2 + q % 2

        @block.sync
        def _(sp):
            sp.dma_start(idt[:], ident).then_inc(s_c, 16)
            sp.dma_start(gb[:], bcast_rows(norm_g, D)).then_inc(s_c, 16)
            sp.dma_start(mi[:, 0], rows(mix, 0)).then_inc(s_m[0], 16)
            for n in range(2):
                sp.dma_start(wr[:, n], w_out[:, n * 512:(n + 1) * 512].rearrange("(c p) n -> p c n", p=P)).then_inc(s_w[n], 16)
            sp.dma_start(xb[:, 0], rows(x, 0)).then_inc(s_x[0], 16)
            sp.dma_start(mi[:, 1], rows(mix, 1)).then_inc(s_m[1], 16)
            sp.dma_start(xb[:, 1], rows(x, 1)).then_inc(s_x[1], 16)

            def slot(k, p, stages):
                t = k * 2 + p
                if "A" in stages and "B" in stages and not (isinstance(k, int) and t == TILES - 1):
                    _, p1, t1 = before(k, p, -1)
                    sp.wait_ge(s_a, t)
                    sp.dma_start(mi[:, p1], rows(mix, t1)).then_inc(s_m[p1], 16)
                if "B" in stages:
                    _, p1, t1 = before(k, p, 1)
                    sp.wait_ge(s_h, t1 + 1)
                    sp.dma_start(rows(h_out, t1), hb[:, p1]).then_inc(s_ho[p1], 16)
                    if "A" in stages and not (isinstance(k, int) and t == TILES - 1):
                        _, p2, t2 = before(k, p, -1)
                        sp.dma_start(xb[:, p2], rows(x, t2)).then_inc(s_x[p2], 16)
                if "C" in stages:
                    _, p2, t2 = before(k, p, 2)
                    stop_at(sp, s_sl, t2 + 1, s_pass_sp)
                    for dst, src in ((hTh, sh), (hTl, sl)):
                        sp.dma_start(dst[:, :, bass.ds(t2 * P, P)].rearrange("c k t -> k c t"), raw(src[:, p2])).then_inc(s_ho2[p2], 16)

            pipeline(sp, slot)
            for p in range(2):
                n = (TILES + 1 - p) // 2
                sp.wait_ge(s_ho[p], 16 * n)
                sp.wait_ge(s_ho2[p], 32 * n)

        @block.tensor
        def _(pe):
            pe.wait_ge(s_c, 32)

            def slot(k, p, stages):
                if "A" in stages:
                    t = k * 2 + p
                    pe.wait_ge(s_m[p], 16 * (k + 1))
                    pe.wait_ge(s_ml, t)
                    for c in range(KC):
                        mm = pe.transpose(ta[:, c * P:(c + 1) * P], mi[:, p, c * P:(c + 1) * P], idt[:])
                    mm.then_inc(s_a, 1)
                if "B" in stages:
                    k1, p1, t = before(k, p, 1)
                    pe.wait_ge(s_ml, t + 1)
                    if not isinstance(t, int) or t >= 2:
                        pe.wait_ge(s_h, t - 1)
                    for n in range(2):
                        if isinstance(t, int) and t == 0:
                            pe.wait_ge((s_wl0, s_wl1)[n], 1)
                        for i, (mm_, ww) in enumerate(((mh, wh), (mh, wl), (ml, wh))):
                            for c in range(KC):
                                mm = pe.matmul(pp[:, p1, n * 512:(n + 1) * 512], mm_[:, p1, c], ww[:, n, c],
                                               start=(i == 0 and c == 0), stop=(i == 2 and c == KC - 1))
                    mm.then_inc(s_b, 1)
                if "C" in stages:
                    k2, p2, t = before(k, p, 2)
                    pe.wait_ge(s_hn, t + 1)
                    pe.wait_ge(s_sl, t)
                    for c in range(KC):
                        mm = pe.transpose(tb[:, c * P:(c + 1) * P], hn[:, p2, c * P:(c + 1) * P], idt[:])
                    mm.then_inc(s_t, 1)

            pipeline(pe, slot)

        @block.scalar
        def _(act):
            act.preload_act_table_set("natural_log_exp_and_others")
            for n in range(2):
                act.wait_ge(s_w[n], 16)
                act.activation(wh[:, n], wr[:, n], ACT.Copy).then_inc(s_wh, 1)

            def slot(k, p, stages):
                if "A" in stages:
                    t = k * 2 + p
                    act.wait_ge(s_a, t + 1)
                    if "C" in stages:
                        act.wait_ge(s_b, t - 1)
                    act.activation(mh[:, p], ta[:].rearrange("p (c k) -> p c k", k=P), ACT.Copy).then_inc(s_mh, 1)
                if "C" in stages:
                    k2, p2, t = before(k, p, 2)
                    act.wait_ge(s_t, t + 1)
                    act.wait_ge(s_ho2[p2], 32 * k2)
                    act.activation(sh[:, p2], tb[:].rearrange("p (c k) -> p c k", k=P), ACT.Copy).then_inc(s_sh, 1)
                if "B" in stages:
                    k1, p1, t = before(k, p, 1)
                    act.wait_ge(s_h, t + 1)
                    if not isinstance(t, int) or t >= 2:
                        act.wait_ge(s_t, t - 1)
                    act.activation(hn[:, p1], hb[:, p1], ACT.Square, accum_out=ss[:, p1, 0:1]).then_inc(s_sq, 1)

            pipeline(act, slot)

        @block.vector
        def _(dve):
            dve.wait_ge(s_wh, 1)
            dve.tensor_tensor(wl[:, 0], wr[:, 0], raw(wh[:, 0]), ALU.subtract).then_inc(s_wl0, 1)
            dve.wait_ge(s_c, 32)

            def slot(k, p, stages):
                if "A" in stages:
                    t = k * 2 + p
                    dve.wait_ge(s_mh, t + 1)
                    dve.tensor_tensor(ml[:, p], ta[:].rearrange("p (c k) -> p c k", k=P), raw(mh[:, p]), ALU.subtract).then_inc(s_ml, 1)
                if "C" in stages:
                    k2, p2, t = before(k, p, 2)
                    dve.wait_ge(s_sh, t + 1)
                    dve.tensor_tensor(sl[:, p2], tb[:].rearrange("p (c k) -> p c k", k=P), raw(sh[:, p2]), ALU.subtract).then_inc(s_sl, 1)
                if "B" in stages:
                    k1, p1, t = before(k, p, 1)
                    dve.wait_ge(s_b, t + 1)
                    dve.wait_ge(s_x[p1], 16 * (k1 + 1))
                    dve.wait_ge(s_ho[p1], 16 * k1)
                    dve.tensor_tensor(hb[:, p1], pp[:, p1], xb[:, p1], ALU.add).then_inc(s_h, 1)
                    dve.wait_ge(s_r, t + 1)
                    dve.scalar_tensor_tensor(out=hn[:, p1], in0=hb[:, p1], scalar=ss[:, p1, 2:3], in1=gb[:],
                                             op0=ALU.mult, op1=ALU.mult).then_inc(s_hn, 1)

            pipeline(dve, slot)

        @block.gpsimd
        def _(pool):
            pool.memset(half_pow[:], -0.5).then_inc(s_cs, 1)
            pool.wait_ge(s_cs, 1)
            pool.wait_ge(s_wh, 2)
            pool.tensor_tensor(wl[:, 1], wr[:, 1], raw(wh[:, 1]), ALU.subtract).then_inc(s_wl1, 1)

            def slot(k, p, stages):
                if "B" in stages:
                    k1, p1, t = before(k, p, 1)
                    stop_at(pool, s_sq, t + 1, s_pass_pool)
                    pool.tensor_scalar(ss[:, p1, 1:2], ss[:, p1, 0:1], 1.0 / D, EPS, ALU.mult, ALU.add).then_inc(s_ms, 1)
                    pool.wait_ge(s_ms, t + 1)
                    pool.tensor_tensor(ss[:, p1, 2:3], ss[:, p1, 1:2], half_pow[:], ALU.pow).then_inc(s_r, 1)

            pipeline(pool, slot)


FG = 256
FC = FG // P
NFG = D_FF // FG


def phase_mlp(nc, hTh, hTl, h, w_up, w_down, y):
    NB = FULL_BLOCKS + 1
    nts = [BT] * FULL_BLOCKS + [LAST_BT]
    W = LAST_BT * P
    with Pool(nc, "ml") as m:
        xh = m.sb("xh", [P, 2, KC, W], F32R)
        xl = m.sb("xl", [P, 2, KC, W], F32R)
        ya = m.sb("ya", [P, LAST_BT, D])
        ur = m.sb("ur", [P, KC, FG])
        uh = m.sb("uh", [P, 2, KC, FG], F32R)
        ul = m.sb("ul", [P, 2, KC, FG], F32R)
        dr = m.sb("dr", [P, FC, D])
        dh = m.sb("dh", [P, 2, FC, D], F32R)
        dl = m.sb("dl", [P, 2, FC, D], F32R)
        r = m.sb("r", [P, FC, W])
        th = m.sb("th", [P, 2, FC, W], F32R)
        tl = m.sb("tl", [P, 2, FC, W], F32R)
        pu = m.ps("pu", [P, FC, 2, 512])
        pd = m.ps("pd", [P, 2, D])
        names = ("ur", "dr", "uh", "ul", "dh", "dl", "up", "r", "sq", "th", "tl", "dn", "ya")
        s_ur, s_dr, s_uh, s_ul, s_dh, s_dl, s_up, s_r, s_sq, s_th, s_tl, s_dn, s_ya = [m.sem(n) for n in names]
        s_hx = m.sems("hx", 2)
        s_y, s_yo = m.sems("y", LAST_BT), m.sems("yo", LAST_BT)
        block = m.block()
        CRED = LAST_BT

        def steps(eng, step, enter=lambda b: None, leave=lambda b: None):
            for b in range(NB):
                enter(b)
                with eng.Fori(0, NFG // 2 - 2) as i:
                    step(b, 2 * i, 0)
                    step(b, 2 * i + 1, 1)
                for g in range(NFG - 4, NFG):
                    step(b, g, g % 2)
                leave(b)

        def ahead(b, g, n):
            if isinstance(g, int):
                b, g = b + (g + n) // NFG, (g + n) % NFG
                return (b, g) if b < NB else None
            return b, g + n

        def number(b, g):
            return g + b * NFG

        def tile_no(b, g, j):
            return g * nts[b] + (b * NFG * BT + j)

        @block.sync
        def _(sp):
            def load_up(b, g):
                sp.wait_ge(s_ul, number(b, g))
                sp.dma_start(ur[:], w_up[:, bass.ds(g * FG, FG)].rearrange("(c p) n -> p c n", p=P)).then_inc(s_ur, 16)

            def load_down(b, g):
                sp.wait_ge(s_dl, number(b, g))
                sp.dma_start(dr[:], w_down[bass.ds(g * FG, FG), :].rearrange("(c p) n -> p c n", p=P)).then_inc(s_dr, 16)

            def load_rows(b):
                n = nts[b] * P
                for dst, src in ((xh, hTh), (xl, hTl)):
                    sp.dma_start(raw(dst[:, b % 2, :, 0:n]), src[:, :, b * BT * P:b * BT * P + n].rearrange("c k t -> k c t")).then_inc(s_hx[b % 2], 16)

            def load_y(b, j):
                sp.dma_start(ya[:, j], rows(h, b * BT + j)).then_inc(s_y[j], 16)

            load_rows(0)
            load_up(0, 0)
            load_up(0, 1)
            load_down(0, 0)
            for j in range(nts[0]):
                load_y(0, j)
            load_up(0, 2)
            load_down(0, 1)

            def enter(b):
                if b + 1 < NB:
                    sp.wait_ge(s_up, b * NFG * FC)
                    load_rows(b + 1)

            def step(b, g, p):
                n = ahead(b, g, 3)
                if n:
                    load_up(*n)
                n = ahead(b, g, 2)
                if n:
                    load_down(*n)

            def leave(b):
                for j in range(nts[b]):
                    t = b * BT + j
                    sp.wait_ge(s_ya, tile_no(b, NFG - 1, j) + 1 + CRED)
                    n = DEC if t == TILES - 1 else P
                    sp.dma_start(y[t * P:t * P + n, :], ya[0:n, j]).then_inc(s_yo[j], 16)
                if b + 1 < NB:
                    for j in range(nts[b + 1]):
                        if j < nts[b]:
                            sp.wait_ge(s_yo[j], 16 * (b + 1))
                        load_y(b + 1, j)

            steps(sp, step, enter, leave)
            for j in range(LAST_BT):
                sp.wait_ge(s_yo[j], 16 * (NB if j < BT else 1))

        @block.tensor
        def _(pe):
            def up(b, g, p):
                G = number(b, g)
                n = nts[b] * P
                cuts = [(0, 0, n)] if n <= 512 else [(0, 0, n // 2), (1, n // 2, n // 2)]
                pe.wait_ge(s_ul, G + 1)
                pe.wait_ge(s_r, G * FC)
                for f in range(FC):
                    for i, (w, xx) in enumerate(((uh, xh), (uh, xl), (ul, xh))):
                        for c in range(KC):
                            for bank, at, size in cuts:
                                mm = pe.matmul(pu[:, f, bank, 0:size], w[:, p, c, f * P:(f + 1) * P], xx[:, b % 2, c, at:at + size],
                                               start=(i == 0 and c == 0), stop=(i == 2 and c == KC - 1))
                    mm.then_inc(s_up, 1)

            def down(b, g, p):
                G = number(b, g)
                pe.wait_ge(s_dl, G + 1)
                pe.wait_ge(s_tl, (G + 1) * FC)
                for j in range(nts[b]):
                    pe.wait_ge(s_ya, tile_no(b, g, j) - 1 + CRED)
                    q = (p * nts[b] + j) % 2
                    for n in range(2):
                        for i, (tt, w) in enumerate(((th, dh), (th, dl), (tl, dh))):
                            for f in range(FC):
                                mm = pe.matmul(pd[:, q, n * 512:(n + 1) * 512], tt[:, p, f, j * P:(j + 1) * P],
                                               w[:, p, f, n * 512:(n + 1) * 512],
                                               start=(i == 0 and f == 0), stop=(i == 2 and f == FC - 1))
                    mm.then_inc(s_dn, 1)

            pe.wait_ge(s_hx[0], 32)
            up(0, 0, 0)

            def step(b, g, p):
                n = ahead(b, g, 1)
                if n:
                    if n[0] != b:
                        pe.wait_ge(s_hx[n[0] % 2], 32 * (n[0] // 2 + 1))
                    up(*n, 1 - p)
                down(b, g, p)

            steps(pe, step)

        @block.scalar
        def _(act):
            act.preload_act_table_set("natural_log_exp_and_others")

            def split_up(b, g, p):
                G = number(b, g)
                act.wait_ge(s_ur, (G + 1) * 16)
                if not (isinstance(g, int) and b == 0 and g < 2):
                    act.wait_ge(s_up, (G - 1) * FC)
                act.activation(uh[:, p], ur[:], ACT.Copy).then_inc(s_uh, 1)

            def split_down(b, g, p):
                G = number(b, g)
                act.wait_ge(s_dr, (G + 1) * 16)
                if not (isinstance(g, int) and b == 0 and g == 0):
                    before_last(act, b, g)
                act.activation(dh[:, p], dr[:], ACT.Copy).then_inc(s_dh, 1)

            def before_last(eng, b, g):
                if isinstance(g, int) and g < 1:
                    eng.wait_ge(s_dn, tile_no(b - 1, NFG - 1, 0))
                else:
                    eng.wait_ge(s_dn, tile_no(b, g - 1, 0))

            def hidden(b, g, p):
                G = number(b, g)
                n = nts[b] * P
                for f in range(FC):
                    src = pu[:, f, 0, 0:n] if n <= 512 else pu[:, f, :, 0:n // 2]
                    dst = r[:, f, 0:n] if n <= 512 else r[:, f, 0:n].rearrange("p (a k) -> p a k", a=2)
                    act.wait_ge(s_up, G * FC + f + 1)
                    act.wait_ge(s_tl, G * FC)
                    act.activation(dst, src, ACT.Relu).then_inc(s_r, 1)
                for f in range(FC):
                    act.wait_ge(s_r, G * FC + f + 1)
                    if not (isinstance(g, int) and b == 0 and g < 2):
                        if f == 0:
                            before_last(act, b, g)
                    act.activation(th[:, p, f, 0:n], r[:, f, 0:n], ACT.Square).then_inc(s_th, 1)

            split_up(0, 0, 0)
            split_up(0, 1, 1)
            split_down(0, 0, 0)
            hidden(0, 0, 0)

            def step(b, g, p):
                n = ahead(b, g, 2)
                if n:
                    split_up(*n, p)
                n = ahead(b, g, 1)
                if n:
                    split_down(*n, 1 - p)
                    hidden(*n, 1 - p)

            steps(act, step)

        @block.gpsimd
        def _(pool):
            def split_up(b, g, p):
                pool.wait_ge(s_uh, number(b, g) + 1)
                pool.tensor_tensor(ul[:, p], ur[:], raw(uh[:, p]), ALU.subtract).then_inc(s_ul, 1)

            split_up(0, 0, 0)
            split_up(0, 1, 1)

            def step(b, g, p):
                n = ahead(b, g, 2)
                if n:
                    split_up(*n, p)

            steps(pool, step)

        @block.vector
        def _(dve):
            dve.sem_inc(s_ya, CRED)

            def split_down(b, g, p):
                dve.wait_ge(s_dh, number(b, g) + 1)
                dve.tensor_tensor(dl[:, p], dr[:], raw(dh[:, p]), ALU.subtract).then_inc(s_dl, 1)

            def hidden(b, g, p):
                G = number(b, g)
                n = nts[b] * P
                for f in range(FC):
                    dve.wait_ge(s_th, G * FC + f + 1)
                    dve.tensor_tensor(r[:, f, 0:n], r[:, f, 0:n], r[:, f, 0:n], ALU.mult).then_inc(s_sq, 1)
                for f in range(FC):
                    dve.wait_ge(s_sq, G * FC + f + 1)
                    dve.tensor_tensor(tl[:, p, f, 0:n], r[:, f, 0:n], raw(th[:, p, f, 0:n]), ALU.subtract).then_inc(s_tl, 1)

            def add(b, g, p):
                for j in range(nts[b]):
                    k = tile_no(b, g, j)
                    dve.wait_ge(s_dn, k + 1)
                    dve.wait_ge(s_y[j], 16 * (b + 1) if j < BT else 16)
                    dve.wait_ge(s_ya, k - nts[b] + 1 + CRED)
                    q = (p * nts[b] + j) % 2
                    dve.tensor_tensor(ya[:, j], ya[:, j], pd[:, q], ALU.add).then_inc(s_ya, 1)

            split_down(0, 0, 0)
            hidden(0, 0, 0)

            def step(b, g, p):
                n = ahead(b, g, 1)
                if n:
                    split_down(*n, 1 - p)
                    hidden(*n, 1 - p)
                add(b, g, p)

            steps(dve, step)


def gla_constants(np):
    j, t = np.arange(P)[:, None], np.arange(P)[None, :]
    same = j // CHUNK == t // CHUNK
    cols, masks = [], []
    for half in LEVELS:
        block = t // (2 * half) * (2 * half)
        mid = block + half
        is_right = t >= mid
        cols.append(np.where(is_right, (j >= mid) & (j <= t), (j > t) & (j < mid)))
        rights = np.arange(P)[(np.arange(P) // half) % 2 == 1][None, :]
        masks.append((j // (2 * half) == rights // (2 * half)) & ((j // half) % 2 == 0))
    cols.append(same & (j <= t))
    masks.append(j == t)
    end = same & (j > t)
    return [np.ascontiguousarray(a, np.float32) for a in (np.concatenate(cols, 1), end, np.concatenate(masks, 1))]


def layer(nc, x, ck, cv, state_in, norm1, w_in, w_a2, b_a2, qg, kg, gla_g, w_out, norm2, w_up, w_down,
          ident, diag_mask, sum_mats, end_mat, score_mask, y, new_k, new_v, new_state):
    def scratch(name, *shape):
        return nc.dram_tensor(name, shape, F32, kind="Internal").ap()

    qT = scratch("q_t", SB_HEADS, P, ROWS)
    kT = scratch("k_t", SB_HEADS, P, KEYS)
    vS = scratch("v_split", KEYS, 2 * SB_HEADS * HD)
    gqk, gv = scratch("gla_qk", ROWS, 512), scratch("gla_v", ROWS, 512)
    sgate, la = scratch("gate", ROWS, 512), scratch("log_a", ROWS, 256)
    mix, h = scratch("mix", ROWS, D), scratch("h", ROWS, D)
    hTh, hTl = scratch("h_t_hi", KC, P, ROWS), scratch("h_t_lo", KC, P, ROWS)

    phase_cache(nc, ck, cv, ident, kT, vS)
    phase_project(nc, x, norm1, w_in, w_a2, b_a2, qg, kg, ident, qT, kT, vS, new_k, new_v, gqk, gv, sgate, la)
    phase_gla(nc, gqk, gv, sgate, la, gla_g, state_in, ident, sum_mats, end_mat, score_mask, mix, new_state)
    phase_attention(nc, qT, kT, vS, ident, diag_mask, mix)
    phase_output(nc, mix, x, w_out, norm2, ident, h, hTh, hTl)
    phase_mlp(nc, hTh, hTl, h, w_up, w_down, y)


def kernel(**inputs):
    import numpy as _np
    import concourse.bacc as _bacc
    from concourse import mybir as _mybir
    from concourse.bass_utils import run_bass_kernel_spmd as _run

    x = _np.concatenate([inputs["x_prompt"][0], inputs["x_sample"][0], _np.zeros((P - DEC, D), _np.float32)], 0)
    arrays = {"x": x, "cache_k": inputs["cache_sb_k"][0, 0], "cache_v": inputs["cache_sb_v"][0, 0],
              "state_in": inputs["state_gla"][0, 0]}
    for name in ("norm1_g", "w_in", "w_a2", "b_a2", "q_norm_g", "k_norm_g", "gla_norm_g", "w_out", "norm2_g", "w_up", "w_down"):
        arrays[name] = inputs[name][0]
    arrays["b_a2"] = arrays["b_a2"].reshape(1, -1)
    sum_mats, end_mat, score_mask = gla_constants(_np)
    arrays["ident"] = _np.eye(P, dtype=_np.float32)
    k = _np.arange(P)
    arrays["diag_mask"] = _np.where(k[None, :] >= k[:, None], _np.float32(NEG), _np.float32(0)).astype(_np.float32)
    arrays["sum_mats"], arrays["end_mat"], arrays["score_mask"] = sum_mats, end_mat, score_mask

    nc = _bacc.Bacc("TRN2", target_bir_lowering=False, num_devices=1)
    arrays = {f"in_{name}": _np.ascontiguousarray(a) for name, a in arrays.items()}
    args = [nc.dram_tensor(name, a.shape, _mybir.dt.from_np(a.dtype), kind="ExternalInput").ap() for name, a in arrays.items()]
    outs = {"y": (SEQ + DEC, D), "new_k": (SEQ + DEC, 512), "new_v": (SEQ + DEC, 512), "new_state": (2, GLA_HEADS, DK, DV)}
    for name, shape in outs.items():
        args.append(nc.dram_tensor(f"out_{name}", shape, F32, kind="ExternalOutput").ap())
    layer(nc, *args)
    got = _run(nc, [arrays], core_ids=[0]).results[0]
    yy, nk, nv, st = [got[f"out_{name}"] for name in outs]

    def heads(a):
        return a.reshape(1, 1, -1, SB_HEADS, HD)

    return (yy[None, :SEQ], yy[None, SEQ:], heads(nk[:SEQ]), heads(nv[:SEQ]), st[0][None, None],
            heads(nk[SEQ:]), heads(nv[SEQ:]), st[1][None, None])
```

```python
from contextlib import ExitStack

import concourse.bass as bass
from concourse import mybir

F32 = mybir.dt.float32
F32R = mybir.dt.float32r
ALU = mybir.AluOpType
ACT = mybir.ActivationFunctionType
AX = mybir.AxisListType

P = 128
D = 1024
KC = D // P
SEQ, DEC, PAST = 2048, 64, 512
TILES = SEQ // P + 1
ROWS = TILES * P
KEYS = SEQ + PAST + P
NEW_KEY_COL = SEQ + PAST
GLA_HEADS, DK, DV = 4, 64, 128
SB_HEADS, HD = 8, 64
RANK = 16
GATE_NORM = 16.0
D_FF = 4 * D
EPS = 1e-6
NEG = -(2.0 ** 100)
CHUNK = 64
LEVELS = (32, 16, 8, 4, 2, 1)

C_GQK, C_GV, C_GATE, C_ALR, C_SQ, C_SK, C_SV = 0, 512, 1024, 1536, 1552, 2064, 2576
GROUP_COLS = (C_SQ, C_SK, C_SV, C_GATE, C_GQK, C_GV)
NG = len(GROUP_COLS)
FULL_BLOCKS = 3
BT = 4
LAST_BT = TILES - FULL_BLOCKS * BT


class Pool:

    def __init__(self, nc, tag):
        self.nc, self.tag, self.ctx, self.semaphores = nc, tag, ExitStack(), []

    def __enter__(self):
        return self

    def __exit__(self, *a):
        done = self.ctx.__exit__(*a)
        if self.semaphores:
            self.nc.clear_and_free_semaphores(self.semaphores)
            self.nc.all_engine_barrier()
        return done

    def sb(self, name, shape, dt=F32):
        return self.ctx.enter_context(self.nc.sbuf_tensor(f"{self.tag}_{name}", shape, dt))

    def ps(self, name, shape, dt=F32):
        return self.ctx.enter_context(self.nc.psum_tensor(f"{self.tag}_{name}", shape, dt))

    def sem(self, name):
        self.semaphores.append(self.nc.alloc_semaphore(f"{self.tag}_{name}"))
        return self.semaphores[-1]

    def sems(self, name, n):
        return [self.sem(f"{name}{i}") for i in range(n)]

    def block(self):
        return self.ctx.enter_context(self.nc.Block())


def raw(ap):
    return ap.bitcast(F32)


def stop_at(eng, sem, value, passed):
    eng.wait_ge(sem, value)
    eng.sem_inc(passed, 1)


def bcast_rows(ap, n):
    return bass.AP(tensor=ap.tensor, offset=ap.offset, ap=[[0, P], [1, n]])


def rows(ap, t, n=1):
    return ap[bass.ds(t * P, n * P), :]


def blocks_loop(eng, body):
    with eng.Fori(0, FULL_BLOCKS) as b:
        body(b, BT, False)
    body(FULL_BLOCKS, LAST_BT, True)


def phase_project(nc, x, cache_k, norm_g, w_in, w_a2, b_a2, qg, kg, ident, qT, kT, new_k, new_v, gqk, gv, sgate, la):
    with Pool(nc, "pj") as m:
        idt = m.sb("idt", [P, P])
        gb = m.sb("gb", [P, D])
        g64 = m.sb("g64", [P, 2, HD])
        wa2 = m.sb("wa2", [32, 256])
        half_pow = m.sb("half_pow", [P, SB_HEADS])
        xb = m.sb("xb", [P, 2, D])
        xn = m.sb("xn", [P, 2, D])
        ssx = m.sb("ssx", [P, 2, 3])
        xh = m.sb("xh", [P, KC, LAST_BT * P], F32R)
        xl = m.sb("xl", [P, KC, LAST_BT * P], F32R)
        wr = m.sb("wr", [P, KC, 512])
        wh = m.sb("wh", [P, 2, KC, 512], F32R)
        wl = m.sb("wl", [P, 2, KC, 512], F32R)
        wah = m.sb("wah", [P, KC, P], F32R)
        wal = m.sb("wal", [P, KC, P], F32R)
        alrT = m.sb("alrT", [32, LAST_BT * P])
        lt = m.sb("lt", [P, 2, 256])
        ld = m.sb("ld", [P, 2, 256])
        tmp = m.sb("tmp", [P, 2, 512])
        ss8 = m.sb("ss8", [P, 2, SB_HEADS])
        ms8 = m.sb("ms8", [P, 2, SB_HEADS])
        r8 = m.sb("r8", [P, 2, SB_HEADS])
        nq = m.sb("nq", [P, 2, 512])
        kn = m.sb("kn", [P, 2, 512])
        vn = m.sb("vn", [P, 2, 512])
        stk = m.sb("stk", [P, 2, SB_HEADS, 2, HD], F32R)
        stT = m.sb("stT", [P, 2, SB_HEADS, P], F32R)
        ng = m.sb("ng", [P, 2, 512])
        ge = m.sb("ge", [P, 2, 512])
        war = tmp[:].rearrange("p a (c n) -> p (a c) n", n=P)
        NC = PAST // P
        ck = [b[:].rearrange("p t (h d) -> p t h d", d=HD) for b in (ng, ge)]
        cks = wh[:, 1].rearrange("p c n -> p (c n)").rearrange("p (t h a d) -> p t h a d", t=NC, a=2, d=HD)
        pj = m.ps("pj", [P, 4, 512])
        tx = m.ps("tx", [P, 2, 512])
        tT = m.ps("tT", [P, 2, 512])

        s_c, s_cs = m.sem("consts"), m.sem("consts_set")
        s_x, s_sq, s_r1, s_rx, s_xn = m.sems("x", 2), m.sem("sq"), m.sem("r1"), m.sem("rx"), m.sem("xn")
        s_tx, s_txf, s_xh = m.sem("tx"), m.sem("txf"), m.sem("xh")
        s_wa, s_wah, s_wal = m.sem("wa"), m.sem("wah"), m.sem("wal")
        s_wr, s_wh, s_wl = m.sems("wr", 2), m.sem("wh"), m.sem("wl")
        s_ae, s_la = m.sem("ae"), m.sems("la", 2)
        s_pj, s_bank = m.sem("pj"), m.sem("bank")
        s_qs, s_qr, s_qp, s_qq, s_qg, s_qh, s_ql, s_tT, s_ev = [m.sem(n) for n in
            ("qs", "qr", "qp", "qq", "qg", "qh", "ql", "tT", "ev")]
        s_kd, s_sd = m.sems("kd", 2), m.sems("sd", 2)
        s_vd = m.sems("vd", 2)
        s_pass, s_passed = m.sem("pass"), m.sem("passed")
        s_ge, s_gp, s_gr, s_ngd = m.sem("ge"), m.sem("gp"), m.sem("gr"), m.sems("ngd", 2)
        s_ckh, s_ckl, s_ckt, s_cke = [m.sem(n) for n in ("ckh", "ckl", "ckt", "cke")]
        s_ck = m.sems("ck", NC // 2)
        s_cko = m.sems("cko", 2)
        block = m.block()

        Q_, K_, V_, GATE_, LAST_ = 0, 1, 2, 3, 5
        TX_USES = 3 * BT + 2
        BANKS, RING = 4, 2

        def slots(nt):
            return [(g, j) for g in range(NG) for j in range(nt)]

        @block.sync
        def _(sp):
            sp.dma_start(idt[:], ident).then_inc(s_c, 16)
            sp.dma_start(gb[:], bcast_rows(norm_g, D)).then_inc(s_c, 16)
            sp.dma_start(g64[:, 0], bcast_rows(qg, HD)).then_inc(s_c, 16)
            sp.dma_start(g64[:, 1], bcast_rows(kg, HD)).then_inc(s_c, 16)
            sp.dma_start(wa2[0:RANK, :], w_a2).then_inc(s_c, 16)
            sp.dma_start(wa2[RANK:RANK + 1, :], b_a2).then_inc(s_c, 16)

            def load_x(b, j):
                sp.wait_ge(s_xn, b * BT + j + 1)
                sp.dma_start(xb[:, j % 2], rows(x, b * BT + j)).then_inc(s_x[j % 2], 16)

            def load_w(b, g, first=False):
                for a in range(2):
                    if not first:
                        sp.wait_ge(s_wl, b * 2 * NG + 2 * g - 1 + a)
                    sp.dma_start(wr[:, 4 * a:4 * a + 4], w_in[a * D // 2:(a + 1) * D // 2, GROUP_COLS[g]:GROUP_COLS[g] + 512]
                                 .rearrange("(c p) n -> p c n", p=P)).then_inc(s_wr[a], 16)

            load_x(0, 0)
            load_x(0, 1)
            sp.wait_ge(s_cs, 3)
            sp.dma_start(war[:, :, 0:RANK], w_in[:, C_ALR:C_ALR + RANK].rearrange("(c p) n -> p c n", p=P)).then_inc(s_wa, 16)
            for k in range(NC // 2):
                sp.dma_start(ck[k], cache_k[2 * k * P:2 * (k + 1) * P].rearrange("(t p) h d -> p t h d", p=P)).then_inc(s_ck[k], 16)
            load_w(0, 0, first=True)
            load_x(0, 2)
            load_x(0, 3)
            for t in range(NC):
                sp.wait_ge(s_cke, 2 * t + 2)
                sp.dma_start(kT[:, :, SEQ + t * P:SEQ + (t + 1) * P].rearrange("h p k -> p h k"),
                             raw(stT[:, t % 2])).then_inc(s_cko[t % 2], 16)
            load_w(0, 1)

            def body(b, nt, last):
                for j in range(BT, nt):
                    load_x(b, j)
                for j in range(nt):
                    sp.wait_ge(s_txf, b * TX_USES + 2 * nt + 2 + j + 1 + RING)
                    sp.dma_start(rows(la, b * BT + j), ld[:, j % 2]).then_inc(s_la[j % 2], 16)
                items = slots(nt)
                for n in range(len(items) + 2):
                    if n < len(items) and items[n][1] == 1:
                        g = items[n][0]
                        if g + 2 < NG:
                            load_w(b, g + 2)
                        elif not last:
                            load_w(b + 1, g + 2 - NG)
                    if n < len(items) and not last:
                        g, j = items[n]
                        if g == LAST_ - 1 and j >= BT - 2:
                            load_x(b + 1, j - (BT - 2))
                        if g == LAST_ and 1 <= j < 3:
                            load_x(b + 1, j + 1)
                    if 1 <= n <= len(items):
                        g, j = items[n - 1]
                        sample = last and j == nt - 1
                        row = b * BT + j
                        drained = b * NG * BT + n + BANKS
                        if g == K_:
                            sp.wait_ge(s_qg, b * 2 * BT + nt + j + 1)
                            sp.dma_start(new_k[SEQ:SEQ + DEC, :] if sample else rows(new_k, row),
                                         kn[0:DEC, j % 2] if sample else kn[:, j % 2]).then_inc(s_kd[j % 2], 16)
                        elif g == V_:
                            sp.wait_ge(s_bank, drained)
                            sp.dma_start(new_v[SEQ:SEQ + DEC, :] if sample else rows(new_v, row),
                                         vn[0:DEC, j % 2] if sample else vn[:, j % 2]).then_inc(s_vd[j % 2], 16)
                        elif g > V_:
                            q = (g - 3) * nt + j
                            sp.wait_ge(s_bank, drained)
                            sp.dma_start(rows((sgate, gqk, gv)[g - 3], row), ng[:, q % 2]).then_inc(s_ngd[q % 2], 16)
                    if n >= 2:
                        g, j = items[n - 2]
                        if g <= K_:
                            q = g * nt + j
                            stop_at(sp, s_ev, (b * 2 * BT + q + 1) * 2 + RING, s_passed)
                            col = NEW_KEY_COL if g == K_ and last and j == nt - 1 else (b * BT + j) * P
                            sp.dma_start((qT, kT)[g][:, :, bass.ds(col, P)].rearrange("h p k -> p h k"),
                                         raw(stT[:, q % 2])).then_inc(s_sd[q % 2], 16)

            blocks_loop(sp, body)
            for q in range(2):
                for s, per_tile in ((s_la, 1), (s_kd, 1), (s_vd, 1), (s_sd, 2), (s_ngd, 3)):
                    sp.wait_ge(s[q], 16 * ((per_tile * TILES + 1 - q) // 2))

        @block.gpsimd
        def _(pool):
            pool.memset(half_pow[:], -0.5).then_inc(s_cs, 1)
            pool.memset(war, 0.0).then_inc(s_cs, 1)
            pool.memset(alrT[:], 1.0).then_inc(s_cs, 1)
            pool.wait_ge(s_c, 96)
            pool.tensor_scalar(g64[:, 0], g64[:, 0], HD ** -0.5, 1.0, ALU.mult, ALU.mult).then_inc(s_cs, 1)
            pool.wait_ge(s_cs, 4)

            def inverse_rms(b, j):
                t = b * BT + j
                stop_at(pool, s_sq, t + 1, s_pass)
                pool.tensor_scalar(ssx[:, j % 2, 1:2], ssx[:, j % 2, 0:1], 1.0 / D, EPS, ALU.mult, ALU.add).then_inc(s_r1, 1)
                pool.wait_ge(s_r1, t + 1)
                pool.tensor_tensor(ssx[:, j % 2, 2:3], ssx[:, j % 2, 1:2], half_pow[:, 0:1], ALU.pow).then_inc(s_rx, 1)

            for j in range(BT):
                inverse_rms(0, j)
                if j == 1:
                    pool.wait_ge(s_wah, 1)
                    pool.tensor_tensor(wal[:], war, raw(wah[:]), ALU.subtract).then_inc(s_wal, 1)

            def body(b, nt, last):
                for j in range(BT, nt):
                    inverse_rms(b, j)
                items = slots(nt)
                for n in range(len(items) + 1):
                    if n >= 1:
                        g, j = items[n - 1]
                        if g <= K_:
                            q = g * nt + j
                            c = b * 2 * BT + q
                            pool.wait_ge(s_bank, b * NG * BT + n + BANKS)
                            out = nq
                            if g == K_:
                                out = kn
                                pool.wait_ge(s_kd[j % 2], 16 * (b * BT // 2 + j // 2))
                                pool.wait_ge(s_ql, c - 1)
                                assert nt + j - 1 > 0
                            oo = out[:, (j if g == K_ else q) % 2].rearrange("p (h d) -> p h d", d=HD)
                            pool.tensor_tensor(oo, nq[:, q % 2].rearrange("p (h d) -> p h d", d=HD),
                                               g64[:, g:g + 1].to_broadcast([P, SB_HEADS, HD]), ALU.mult).then_inc(s_qg, 1)
                    if n < len(items):
                        g, j = items[n]
                        if g <= K_:
                            q = g * nt + j
                            c = b * 2 * BT + q
                            stop_at(pool, s_qr, c + 1 + RING, s_pass)
                            pool.tensor_scalar(ms8[:, q % 2], ss8[:, q % 2], 1.0 / HD, EPS, ALU.mult, ALU.add).then_inc(s_qp, 1)
                            pool.wait_ge(s_qp, c + 1)
                            pool.tensor_tensor(r8[:, q % 2], ms8[:, q % 2], half_pow[:], ALU.pow).then_inc(s_qq, 1)
                        elif g == GATE_:
                            stop_at(pool, s_ge, b * BT + j + 1, s_pass)
                            pool.tensor_scalar(ge[:, j % 2], ge[:, j % 2], 1.0, 1.0, ALU.add, ALU.mult).then_inc(s_gp, 1)
                    if n < len(items) and items[n][0] == LAST_ and not last:
                        inverse_rms(b + 1, items[n][1])

            blocks_loop(pool, body)

        @block.scalar
        def _(act):
            act.preload_act_table_set("natural_log_exp_and_others")

            def split_w(b, g, nt):
                act.wait_ge(s_pj, b * NG * BT + ((g - 1) * nt + BT if g > 1 else g * BT))
                for a in range(2):
                    act.wait_ge(s_wr[a], 16 * (b * NG + g + 1))
                    act.activation(wh[:, g % 2, 4 * a:4 * a + 4], wr[:, 4 * a:4 * a + 4], ACT.Copy).then_inc(s_wh, 1)

            def square(b, j):
                t = b * BT + j
                act.wait_ge(s_x[j % 2], 16 * (b * BT // 2 + j // 2 + 1))
                if j >= 2:
                    act.wait_ge(s_tx, b * TX_USES + 2 * (j - 1))
                else:
                    act.wait_ge(s_tx, b * TX_USES)
                act.activation(xn[:, j % 2], xb[:, j % 2], ACT.Square, accum_out=ssx[:, j % 2, 0:1]).then_inc(s_sq, 1)

            def high_halves(b, j):
                act.wait_ge(s_pj, b * NG * BT + min(j + 1, BT))
                for a in range(2):
                    act.wait_ge(s_tx, b * TX_USES + 2 * j + a + 1)
                    act.activation(xh[:, 4 * a:4 * a + 4, j * P:(j + 1) * P],
                                   tx[:, a].rearrange("p (c k) -> p c k", k=P), ACT.Copy).then_inc(s_xh, 1)

            square(0, 0)
            square(0, 1)
            act.wait_ge(s_wa, 16)
            act.activation(wah[:], war, ACT.Copy).then_inc(s_wah, 1)
            for k in range(NC // 2):
                act.wait_ge(s_ck[k], 16)
                act.activation(cks[:, 2 * k:2 * k + 2, :, 0, :], ck[k], ACT.Copy).then_inc(s_ckh, 1)
            for j in range(BT - 1):
                high_halves(0, j)
                if j + 2 < BT:
                    square(0, j + 2)
            for n in range(2 * NC):
                t, a = n // 2, n % 2
                if t >= 2:
                    act.wait_ge(s_cko[t % 2], 16 * (t // 2))
                act.wait_ge(s_ckt, n + 1)
                act.activation(stT[:, t % 2, 4 * a:4 * a + 4, :], tT[:, a].rearrange("p (h k) -> p h k", k=P),
                               ACT.Copy).then_inc(s_cke, 1)
            split_w(0, 0, BT)
            for t in range(2):
                act.wait_ge(s_cko[t], 16 * NC // 2)
            act.wait_ge(s_wal, 1)

            def body(b, nt, last):
                for j in range(BT, nt):
                    square(b, j)
                for j in range(BT - 1, nt):
                    high_halves(b, j)
                for j in range(nt):
                    t = b * BT + j
                    act.wait_ge(s_tx, b * TX_USES + 2 * nt + 2 + j + 1)
                    if j >= 2:
                        act.wait_ge(s_txf, b * TX_USES + 2 * nt + 2 + j - 1 + RING)
                    act.activation(lt[:, j % 2], tx[:, j % 2, 0:256], ACT.Abs).then_inc(s_ae, 1)
                    act.wait_ge(s_ae, 3 * t + 1)
                    act.activation(lt[:, j % 2], lt[:, j % 2], ACT.Exp, scale=-1.0).then_inc(s_ae, 1)
                    act.wait_ge(s_ae, 3 * t + 2)
                    act.activation(lt[:, j % 2], lt[:, j % 2], ACT.Ln, bias=1.0).then_inc(s_ae, 1)
                items = slots(nt)
                for n in range(len(items) + 2):
                    if n < len(items):
                        g, j = items[n]
                        bank = pj[:, n % 4]
                        if g <= K_ or g == GATE_:
                            act.wait_ge(s_pj, b * NG * BT + n + 1 + BT)
                        if g <= K_:
                            q = g * nt + j
                            act.wait_ge(s_qr, b * 2 * BT + q + 1)
                            act.activation(tmp[:, q % 2], bank, ACT.Square).then_inc(s_qs, 1)
                        elif g == GATE_:
                            act.wait_ge(s_bank, b * NG * BT + n - 1 + BANKS)
                            act.activation(ge[:, j % 2], bank, ACT.Exp, scale=-1.0).then_inc(s_ge, 1)
                    if 1 <= n <= len(items):
                        g, j = items[n - 1]
                        if g <= K_:
                            q = g * nt + j
                            c = b * 2 * BT + q
                            act.wait_ge(s_qg, c + 1)
                            act.wait_ge(s_tT, 2 * c)
                            src = kn[:, j % 2] if g == K_ else nq[:, q % 2]
                            act.activation(stk[:, q % 2, :, 0, :], src.rearrange("p (h d) -> p h d", d=HD),
                                           ACT.Copy).then_inc(s_qh, 1)
                    if n >= 2:
                        g, j = items[n - 2]
                        if g <= K_:
                            q = g * nt + j
                            c = b * 2 * BT + q
                            act.wait_ge(s_sd[q % 2], 16 * (b * BT + q // 2))
                            for a in range(2):
                                act.wait_ge(s_tT, 2 * c + a + 1 + RING)
                                act.activation(stT[:, q % 2, 4 * a:4 * a + 4, :],
                                               tT[:, a].rearrange("p (h k) -> p h k", k=P), ACT.Copy).then_inc(s_ev, 1)
                    if n < len(items) and items[n][1] == 0:
                        g = items[n][0]
                        if g + 1 < NG:
                            split_w(b, g + 1, nt)
                        elif not last:
                            split_w(b + 1, 0, BT)
                    if n < len(items) and not last:
                        g, j = items[n]
                        if (g, j) == (LAST_ - 1, BT - 1):
                            square(b + 1, 0)
                        if g == LAST_:
                            if j >= 1:
                                high_halves(b + 1, j - 1)
                            if j + 1 < BT:
                                square(b + 1, j + 1)

            act.sem_inc(s_ev, RING)
            blocks_loop(act, body)

        @block.vector
        def _(dve):
            dve.sem_inc(s_xn, RING)
            dve.sem_inc(s_txf, RING)
            dve.sem_inc(s_bank, BANKS)
            dve.sem_inc(s_qr, RING)

            def split_w(b, g):
                for a in range(2):
                    dve.wait_ge(s_wh, b * 2 * NG + 2 * g + a + 1)
                    c = slice(4 * a, 4 * a + 4)
                    dve.tensor_tensor(wl[:, g % 2, c], wr[:, c], raw(wh[:, g % 2, c]), ALU.subtract).then_inc(s_wl, 1)

            def norm(b, j):
                dve.wait_ge(s_rx, b * BT + j + 1)
                dve.scalar_tensor_tensor(out=xn[:, j % 2], in0=xb[:, j % 2], scalar=ssx[:, j % 2, 2:3], in1=gb[:],
                                         op0=ALU.mult, op1=ALU.mult).then_inc(s_xn, 1)

            def low_halves(b, j):
                for a in range(2):
                    dve.wait_ge(s_xh, 2 * (b * BT + j) + a + 1)
                    dst = xh[:, 4 * a:4 * a + 4, j * P:(j + 1) * P]
                    dve.tensor_tensor(xl[:, 4 * a:4 * a + 4, j * P:(j + 1) * P],
                                      tx[:, a].rearrange("p (c k) -> p c k", k=P), raw(dst), ALU.subtract).then_inc(s_txf, 1)

            dve.wait_ge(s_c, 96)
            for j in range(BT):
                norm(0, j)
                if j == 1:
                    for k in range(NC // 2):
                        t = slice(2 * k, 2 * k + 2)
                        dve.wait_ge(s_ckh, k + 1)
                        dve.tensor_tensor(cks[:, t, :, 1, :], ck[k], raw(cks[:, t, :, 0, :]), ALU.subtract).then_inc(s_ckl, 1)
                if j >= 1:
                    low_halves(0, j - 1)
            split_w(0, 0)

            def body(b, nt, last):
                for j in range(BT, nt):
                    norm(b, j)
                for j in range(BT - 1, nt):
                    low_halves(b, j)
                half = nt * P // 2
                for a in range(2):
                    dve.wait_ge(s_tx, b * TX_USES + 2 * nt + a + 1)
                    dve.tensor_copy(alrT[0:RANK, a * half:(a + 1) * half], tx[0:RANK, a, 0:half]).then_inc(s_txf, 1)
                for j in range(nt):
                    t = b * BT + j
                    dve.wait_ge(s_ae, 3 * t + 3)
                    dve.wait_ge(s_la[j % 2], 16 * (b * BT // 2 + j // 2))
                    dve.scalar_tensor_tensor(out=ld[:, j % 2], in0=tx[:, j % 2, 0:256], scalar=0.0, in1=lt[:, j % 2],
                                             op0=ALU.min, op1=ALU.subtract).then_inc(s_txf, 1)
                items = slots(nt)
                for n in range(len(items) + 1):
                    if n >= 1:
                        g, j = items[n - 1]
                        if g <= K_:
                            q = g * nt + j
                            c = b * 2 * BT + q
                            dve.wait_ge(s_qq, c + 1)
                            dve.tensor_tensor(nq[:, q % 2].rearrange("p (h d) -> p h d", d=HD),
                                              pj[:, (n - 1) % 4].rearrange("p (h d) -> p h d", d=HD),
                                              r8[:, q % 2].unsqueeze(2).to_broadcast([P, SB_HEADS, HD]), ALU.mult).then_inc(s_bank, 1)
                    if n < len(items):
                        g, j = items[n]
                        bank = pj[:, n % 4]
                        if g <= K_:
                            q = g * nt + j
                            dve.wait_ge(s_qs, b * 2 * BT + q + 1)
                            dve.tensor_reduce(ss8[:, q % 2], tmp[:, q % 2].rearrange("p (h d) -> p h d", d=HD),
                                              AX.X, ALU.add).then_inc(s_qr, 1)
                        elif g == V_:
                            dve.wait_ge(s_vd[j % 2], 16 * (b * BT // 2 + j // 2))
                            dve.wait_ge(s_pj, b * NG * BT + n + 1 + BT)
                            dve.tensor_copy(vn[:, j % 2], bank).then_inc(s_bank, 1)
                        else:
                            q = (g - 3) * nt + j
                            dve.wait_ge(s_ngd[q % 2], 16 * (b * 3 * BT // 2 + q // 2))
                            if g == GATE_:
                                dve.wait_ge(s_gp, b * BT + j + 1)
                                dve.reciprocal(ge[:, j % 2], ge[:, j % 2]).then_inc(s_gr, 1)
                                dve.wait_ge(s_gr, b * BT + j + 1)
                                dve.tensor_tensor(ng[:, q % 2], bank, ge[:, j % 2], ALU.mult).then_inc(s_bank, 1)
                            else:
                                dve.wait_ge(s_pj, b * NG * BT + n + 1 + BT)
                                dve.tensor_copy(ng[:, q % 2], bank).then_inc(s_bank, 1)
                    if n >= 1:
                        g, j = items[n - 1]
                        if g <= K_:
                            q = g * nt + j
                            dve.wait_ge(s_qh, b * 2 * BT + q + 1)
                            src = kn[:, j % 2] if g == K_ else nq[:, q % 2]
                            dve.tensor_tensor(stk[:, q % 2, :, 1, :], src.rearrange("p (h d) -> p h d", d=HD),
                                              raw(stk[:, q % 2, :, 0, :]), ALU.subtract).then_inc(s_ql, 1)
                    if n < len(items) and items[n][1] == 0:
                        g = items[n][0]
                        if g + 1 < NG:
                            split_w(b, g + 1)
                        elif not last:
                            split_w(b + 1, 0)
                    if n < len(items) and items[n][0] == LAST_ and not last:
                        j = items[n][1]
                        norm(b + 1, j)
                        if j >= 1:
                            low_halves(b + 1, j - 1)

            blocks_loop(dve, body)

        @block.tensor
        def _(pe):
            pe.sem_inc(s_pj, BT)
            pe.sem_inc(s_tT, RING)
            pe.wait_ge(s_c, 96)
            pe.wait_ge(s_cs, 3)

            def transposes(b, j):
                pe.wait_ge(s_xn, b * BT + j + 1 + RING)
                for a in range(2):
                    pe.wait_ge(s_txf, b * TX_USES + 2 * j + a + 1)
                    for c in range(4):
                        k = 4 * a + c
                        mm = pe.transpose(tx[:, a, c * P:(c + 1) * P], xn[:, j % 2, k * P:(k + 1) * P], idt[:])
                    mm.then_inc(s_tx, 1)

            for j in range(BT - 1):
                transposes(0, j)
            pe.wait_ge(s_ckl, NC // 2)
            for n in range(2 * NC):
                t, a = n // 2, n % 2
                if t >= 1:
                    pe.wait_ge(s_cke, n - 1)
                for h in range(4):
                    mm = pe.transpose(tT[:, a, h * P:(h + 1) * P],
                                      raw(cks[:, t, 4 * a + h]).rearrange("p a d -> p (a d)"), idt[:])
                mm.then_inc(s_ckt, 1)
            pe.wait_ge(s_cke, 2 * NC)
            pe.wait_ge(s_wal, 1)

            def body(b, nt, last):
                for j in range(BT - 1, nt):
                    transposes(b, j)
                half = nt * P // 2
                for a in range(2):
                    if a == 0:
                        pe.wait_ge(s_txf, b * TX_USES + 2 * nt + RING)
                    for i, (w, xx) in enumerate(((wah, xh), (wah, xl), (wal, xh))):
                        for k in range(KC):
                            mm = pe.matmul(tx[:, a, 0:half], w[:, k, :], xx[:, k, a * half:(a + 1) * half],
                                           start=(i == 0 and k == 0), stop=(i == 2 and k == KC - 1))
                    mm.then_inc(s_tx, 1)
                for j in range(nt):
                    pe.wait_ge(s_txf, b * TX_USES + 2 * nt + RING + max(2, 1 + j))
                    pe.matmul(tx[:, j % 2, 0:256], alrT[0:RANK + 1, j * P:(j + 1) * P], wa2[0:RANK + 1, :],
                              start=True, stop=True).then_inc(s_tx, 1)
                items = slots(nt)
                for n in range(len(items) + 2):
                    if n < len(items):
                        g, j = items[n]
                        if j == 0:
                            pe.wait_ge(s_wl, b * 2 * NG + 2 * g + 2)
                        pe.wait_ge(s_bank, b * NG * BT + n + 1)
                        ts = slice(j * P, (j + 1) * P)
                        for i, (xx, w) in enumerate(((xh, wh), (xh, wl), (xl, wh))):
                            for k in range(KC):
                                mm = pe.matmul(pj[:, n % 4], xx[:, k, ts], w[:, g % 2, k, :],
                                               start=(i == 0 and k == 0), stop=(i == 2 and k == KC - 1))
                        mm.then_inc(s_pj, 1)
                        if g == LAST_ and j >= 1 and not last:
                            transposes(b + 1, j - 1)
                    if n >= 2:
                        g, j = items[n - 2]
                        if g <= K_:
                            q = g * nt + j
                            c = b * 2 * BT + q
                            pe.wait_ge(s_ql, c + 1)
                            for a in range(2):
                                pe.wait_ge(s_ev, 2 * c + a + 1)
                                for h in range(4):
                                    mm = pe.transpose(tT[:, a, h * P:(h + 1) * P],
                                                      raw(stk[:, q % 2, 4 * a + h]).rearrange("p a d -> p (a d)"), idt[:])
                                mm.then_inc(s_tT, 1)

            blocks_loop(pe, body)


NL = len(LEVELS)
DCOLS = (NL + 1) * P
SCOLS = NL * CHUNK + P


def right(ap, level):
    return ap.rearrange("p (n a l) -> p n a l", a=2, l=LEVELS[level])[:, :, 1, :]


def phase_gla(nc, gqk, gv, sgate, la, gla_g, state_in, ident, sum_mats, end_mat, score_mask, mix, new_state, pad_values, load_first):
    with Pool(nc, "gl") as m:
        idt = m.sb("idt", [P, P])
        ones = m.sb("ones", [P, DCOLS + P])
        am = m.sb("am", [P, DCOLS], F32R)
        ae = m.sb("ae", [P, P], F32R)
        mask = m.sb("mask", [P, SCOLS])
        gb = m.sb("gb", [P, GLA_HEADS, DV])
        half_pow = m.sb("half_pow", [P, GLA_HEADS])
        qk = m.sb("qk", [P, 2, 512])
        lat = m.sb("lat", [P, 2, 256])
        lah = m.sb("lah", [P, 2, 256], F32R)
        lal = m.sb("lal", [P, 2, 256], F32R)
        sg = m.sb("sg", [P, 2, 512])
        v = m.sb("v", [P, 2, 512])
        qkT = m.sb("qkT", [P, 2, 4, P])
        ex = m.sb("ex", [P, 2, 2, DCOLS])
        kx = m.sb("kx", [P, 2, 2, NL, P])
        qx = m.sb("qx", [P, 2, 2, NL, P])
        qb = m.sb("qb", [P, 2, 2, 3 * P])
        ken = m.sb("ken", [P, 2, 256])
        ke = m.sb("ke", [P, 2, 256])
        sm = m.sb("sm", [P, GLA_HEADS, SCOLS])
        st = m.sb("st", [P, 2, 2, 2, DV])
        o2 = m.sb("o2", [P, 512])
        ss4 = m.sb("ss4", [P, GLA_HEADS])
        ms4 = m.sb("ms4", [P, GLA_HEADS])
        r4 = m.sb("r4", [P, GLA_HEADS])
        on = m.sb("on", [P, 512])
        sgg = m.sb("sgg", [P, 3, 512])
        mo = m.sb("mo", [P, 2, 512])
        pt = m.ps("pt", [P, 512])
        pd = m.ps("pd", [P, 2, 512])
        pn = m.ps("pn", [P, 512])
        psc = m.ps("psc", [P, 2, 512])
        po = m.ps("po", [P, 512])
        pu = m.ps("pu", [P, 512])
        names = ("c", "cs", "tr", "trq", "trk", "d", "dx", "kx", "qx", "qb", "n", "nx", "ke", "sgg",
                 "ua", "st", "sc", "sm", "lv", "as", "lh", "ll", "o", "sq", "ss", "ms", "r", "on", "mo")
        (s_c, s_cs, s_tr, s_trq, s_trk, s_d, s_dx, s_kx, s_qx, s_qb, s_n, s_nx, s_ke, s_sgg,
         s_ua, s_st, s_sc, s_sm, s_lv, s_as, s_lh, s_ll, s_o, s_sq, s_ss, s_ms, s_r, s_on, s_mo) = [m.sem(n) for n in names]
        s_in, s_v, s_md = m.sems("in", 2), m.sems("v", 2), m.sems("md", 2)
        s_pass_sp, s_pass_pe, s_pass_pool = m.sem("pass_sp"), m.sem("pass_pe"), m.sem("pass_pool")
        s_am, s_vz, s_hin, s_hv = m.sem("am"), m.sem("vz"), m.sem("hin"), m.sem("hv")
        s_si, s_so, s_sp = m.sem("si"), m.sem("so"), m.sem("sp")
        block = m.block()
        LAST = TILES - 1

        def pipeline(eng, slot):
            slot(0, 0, (1,), False)
            slot(0, 1, (1, 2), False)
            with eng.Fori(0, (LAST - 2) // 2) as i:
                slot(i + 1, 0, (3, 1, 2), False)
                slot(i + 1, 1, (3, 1, 2), False)
            slot(LAST // 2, 0, (3, 1, 2), False)
            slot(LAST // 2, 1, (3, 2), True)
            slot(LAST // 2 + 1, 0, (3,), False)

        def before(h, p, n):
            q = p - n
            h = h + q // 2
            return h, q % 2, h * 2 + q % 2

        @block.sync
        def _(sp):
            sp.dma_start(idt[:], ident).then_inc(s_c, 16)
            sp.dma_start(ones[:, 0:DCOLS], sum_mats).then_inc(s_c, 16)
            sp.dma_start(ones[:, DCOLS:DCOLS + P], end_mat).then_inc(s_c, 16)
            sp.dma_start(mask[:], score_mask).then_inc(s_c, 16)
            for h in range(GLA_HEADS):
                sp.dma_start(gb[:, h], bcast_rows(gla_g, DV)).then_inc(s_c, 16)

            def load(h, p):
                t = h * 2 + p
                for dst, src in ((qk, gqk), (lat, la), (sg, sgate)):
                    sp.dma_start(dst[:, p], rows(src, t)).then_inc(s_in[p], 16)

            load(0, 0)
            load(0, 1)

            def slot(h, p, stages, sample):
                t = h * 2 + p
                if 1 in stages:
                    if 3 in stages:
                        sp.wait_ge(s_o, 4 * (t - 1))
                    sp.dma_start(v[:, p], rows(gv, t)).then_inc(s_v[p], 16)
                if sample:
                    sp.wait_ge(s_st, 4 * LAST)
                    ns = st[:, LAST % 2, 0]
                    sp.dma_start(new_state[0].rearrange("(a b) k v -> (b k) a v", b=2), ns).then_inc(s_so, 16)
                    sp.wait_ge(s_so, 16)
                    sp.dma_start(ns, state_in.rearrange("(a b) k v -> (b k) a v", b=2)).then_inc(s_si, 16)
                if 3 in stages:
                    h2, p2, t2 = before(h, p, 2)
                    sp.wait_ge(s_mo, t2 + 1)
                    sp.dma_start(mix[bass.ds(t2 * P, P), 0:512], mo[:, p2]).then_inc(s_md[p2], 16)
                if 1 in stages and 2 in stages and not (isinstance(h, int) and h * 2 + p >= LAST):
                    sp.wait_ge(s_qb, 2 * t)
                    sp.wait_ge(s_ke, t)
                    stop_at(sp, s_sgg, t, s_pass_sp)
                    h1, p1, t1 = before(h, p, -1)
                    load(h1, p1)
                if isinstance(h, int) and h * 2 + p == 1:
                    sp.wait_ge(s_vz, 1)
                    load_first(sp, s_hin, s_hv)

            pipeline(sp, slot)
            sp.wait_ge(s_hin, 80)
            sp.wait_ge(s_hv, 48)
            sp.wait_ge(s_st, 4 * LAST + 2)
            sp.dma_start(new_state[1].rearrange("(a b) k v -> (b k) a v", b=2), st[:, LAST % 2, 1]).then_inc(s_so, 16)
            sp.wait_ge(s_so, 32)
            sp.wait_ge(s_md[0], 16 * (TILES // 2 + 1))
            sp.wait_ge(s_md[1], 16 * (TILES // 2))

        @block.tensor
        def _(pe):
            pe.wait_ge(s_c, 128)
            pe.wait_ge(s_am, 2)

            def stage1(h, p):
                t = h * 2 + p
                pe.wait_ge(s_in[p], 48 * (h + 1))
                pe.wait_ge(s_trq, t)
                pe.wait_ge(s_trk, t)
                for c in range(4):
                    mm = pe.transpose(pt[:, c * P:(c + 1) * P], qk[:, p, c * P:(c + 1) * P], idt[:])
                mm.then_inc(s_tr, 1)
                pe.wait_ge(s_ll, t + 1)
                for a in range(2):
                    for i, (lo, hi) in enumerate(((0, 512), (512, DCOLS))):
                        pe.wait_ge(s_dx, 4 * t + 2 * a + i - 1 if a or i else 4 * t)
                        pe.matmul(pd[:, i, 0:hi - lo], lah[:, p, a * P:(a + 1) * P], am[:, lo:hi], start=True, stop=False)
                        pe.matmul(pd[:, i, 0:hi - lo], lal[:, p, a * P:(a + 1) * P], am[:, lo:hi],
                                  start=False, stop=True).then_inc(s_d, 1)
                pe.wait_ge(s_nx, t)
                pe.matmul(pn[:, 0:256], ae[:], lah[:, p, :], start=True, stop=False)
                pe.matmul(pn[:, 0:256], ae[:], lal[:, p, :], start=False, stop=True).then_inc(s_n, 1)

            def chunk_update(p, c):
                for hd in range(GLA_HEADS):
                    a, half = hd // 2, slice(64 * (hd % 2), 64 * (hd % 2) + 64)
                    tok = slice(CHUNK * c, CHUNK * c + CHUNK)
                    mm = pe.matmul(pu[half, a * DV:(a + 1) * DV], ke[tok, p, hd * DK:(hd + 1) * DK],
                                   v[tok, p, hd * DV:(hd + 1) * DV], start=True, stop=True)
                mm.then_inc(s_ua, 1)

            def scores(h, p, t, a):
                halves = (slice(0, 64), slice(64, 128))
                pe.wait_ge(s_sm, 4 * t + 2 * a)
                for i in range(NL):
                    for e, half in enumerate(halves):
                        pe.matmul(psc[:, e, i * CHUNK:(i + 1) * CHUNK], kx[half, p, a, i, :], right(qx[half, p, a, i, :], i),
                                  start=True, stop=True)
                for e, half in enumerate(halves):
                    pe.matmul(psc[:, e, NL * CHUNK:SCOLS], qkT[half, p, 2 + a, :], qkT[half, p, a, :],
                              start=True, stop=True).then_inc(s_sc, 1)

            def outputs(h, p, t, hd):
                a, half = hd // 2, slice(64 * (hd % 2), 64 * (hd % 2) + 64)
                dst = po[:, hd * DV:(hd + 1) * DV]
                pe.wait_ge(s_as, 4 * t + hd + 1)
                pe.wait_ge(s_o, 4 * t + hd)
                pe.matmul(dst, sm[:, hd, NL * CHUNK:SCOLS], v[:, p, hd * DV:(hd + 1) * DV], start=True, stop=False)
                pe.matmul(dst, qb[half, p, a, 0:P], st[half, p, 0, a], start=False, stop=False)
                pe.matmul(dst, qb[half, p, a, P:2 * P], st[half, p, 1, a], start=False, stop=True).then_inc(s_o, 1)

            def slot(h, p, stages, sample):
                if 2 in stages:
                    h1, p1, t = before(h, p, 1)
                    pe.wait_ge(s_kx, 2 * t + 1)
                    pe.wait_ge(s_qx, 2 * t + 1)
                    scores(h1, p1, t, 0)
                    pe.wait_ge(s_v[p1], 16 * (h1 + 1))
                    pe.wait_ge(s_ke, t + 1)
                    stop_at(pe, s_st, 4 * t, s_pass_pe)
                    chunk_update(p1, 0)
                    pe.wait_ge(s_kx, 2 * t + 2)
                    pe.wait_ge(s_qx, 2 * t + 2)
                    scores(h1, p1, t, 1)
                    stop_at(pe, s_st, 4 * t + 2, s_pass_pe)
                    chunk_update(p1, 1)
                if 1 in stages:
                    stage1(h, p)
                if 2 in stages:
                    pe.wait_ge(s_on, t)
                    pe.wait_ge(s_qb, 2 * t + 2)
                    if sample:
                        pe.wait_ge(s_si, 16)
                    for hd in range(GLA_HEADS):
                        outputs(h1, p1, t, hd)

            pipeline(pe, slot)

        @block.scalar
        def _(act):
            act.preload_act_table_set("natural_log_exp_and_others")
            act.wait_ge(s_c, 128)
            act.activation(am[:], ones[:, 0:DCOLS], ACT.Copy).then_inc(s_am, 1)
            act.activation(ae[:], ones[:, DCOLS:DCOLS + P], ACT.Copy).then_inc(s_am, 1)

            def slot(h, p, stages, sample):
                if 3 in stages:
                    h2, p2, t2 = before(h, p, 2)
                    act.wait_ge(s_o, 4 * (t2 + 1))
                    act.wait_ge(s_ss, t2)
                    act.activation(o2[:], po[:], ACT.Square).then_inc(s_sq, 1)
                if 1 in stages:
                    t = h * 2 + p
                    act.wait_ge(s_tr, t + 1)
                    if 3 in stages:
                        act.wait_ge(s_o, 4 * (t - 1))
                    act.activation(qkT[:, p, 0:2], pt[:, 0:2 * P].rearrange("p (c k) -> p c k", k=P), ACT.Copy,
                                   scale=DK ** -0.5).then_inc(s_trq, 1)
                    for a in range(2):
                        for i, (lo, hi) in enumerate(((0, 512), (512, DCOLS))):
                            act.wait_ge(s_d, 4 * t + 2 * a + i + 1)
                            act.activation(ex[:, p, a, lo:hi], pd[:, i, 0:hi - lo], ACT.Exp, scale=1.0 / GATE_NORM).then_inc(s_dx, 1)
                    act.wait_ge(s_n, t + 1)
                    act.activation(ken[:, p], pn[:, 0:256], ACT.Exp, scale=1.0 / GATE_NORM).then_inc(s_nx, 1)

            pipeline(act, slot)

        @block.vector
        def _(dve):
            dve.memset(pad_values, 0.0).then_inc(s_vz, 1)
            dve.memset(st[:, 0, 0], 0.0).then_inc(s_sp, 1)
            dve.memset(qb[:], 0.0).then_inc(s_sp, 1)
            dve.wait_ge(s_sp, 2)
            dve.wait_ge(s_c, 128)

            def new_states(h, p, t, c, sample):
                dve.wait_ge(s_ua, 2 * t + c + 1)
                for a in range(2):
                    src = st[:, p, c, a]
                    dst = st[:, p, 1, a] if c == 0 else st[:, 1 - p, 0, a]
                    end = NL * P + CHUNK * c + CHUNK - 1
                    dve.scalar_tensor_tensor(out=dst, in0=src, scalar=ex[:, p, a, end:end + 1], in1=pu[:, a * DV:(a + 1) * DV],
                                             op0=ALU.mult, op1=ALU.add).then_inc(s_st, 1)

            def masked(t, hd):
                dve.wait_ge(s_sc, 4 * t + hd + 1)
                if not isinstance(t, int) or t > 0:
                    dve.wait_ge(s_o, 4 * t + hd - 3)
                dve.tensor_tensor(sm[:, hd], psc[:, hd % 2], mask[:], ALU.mult).then_inc(s_sm, 1)

            def level_sums(t, pair):
                for i in range(NL):
                    for e in range(2):
                        hd = 2 * pair + e
                        if i == 0:
                            dve.wait_ge(s_sm, 4 * t + hd + 1)
                        else:
                            dve.wait_ge(s_lv, (t * 2 + pair) * 2 * (NL - 1) + 2 * (i - 1) + e + 1)
                        whole = sm[:, hd, NL * CHUNK:SCOLS]
                        part = sm[:, hd, i * CHUNK:(i + 1) * CHUNK].rearrange("p (n l) -> p n l", l=LEVELS[i])
                        dve.tensor_tensor(right(whole, i), right(whole, i), part, ALU.add).then_inc(s_as if i == NL - 1 else s_lv, 1)

            def slot(h, p, stages, sample):
                if 2 in stages:
                    h1, p1, t = before(h, p, 1)
                    if sample:
                        dve.wait_ge(s_si, 16)
                    masked(t, 0)
                    masked(t, 1)
                    new_states(h1, p1, t, 0, sample)
                if 3 in stages:
                    h2, p2, t2 = before(h, p, 2)
                    dve.wait_ge(s_sq, t2 + 1)
                    dve.tensor_reduce(ss4[:], o2[:].rearrange("p (h d) -> p h d", d=DV), AX.X, ALU.add).then_inc(s_ss, 1)
                if 2 in stages:
                    level_sums(t, 0)
                if 3 in stages:
                    dve.wait_ge(s_r, t2 + 1)
                    dve.wait_ge(s_mo, t2)
                    dve.tensor_tensor(on[:].rearrange("p (h d) -> p h d", d=DV), po[:].rearrange("p (h d) -> p h d", d=DV),
                                      r4[:].unsqueeze(2).to_broadcast([P, GLA_HEADS, DV]), ALU.mult).then_inc(s_on, 1)
                if 2 in stages:
                    masked(t, 2)
                    masked(t, 3)
                    dve.wait_ge(s_st, 4 * t + 2)
                    new_states(h1, p1, t, 1, sample)
                    level_sums(t, 1)
                if 1 in stages:
                    t = h * 2 + p
                    dve.wait_ge(s_tr, t + 1)
                    dve.wait_ge(s_trq, t + 1)
                    dve.tensor_copy(qkT[:, p, 2:4], pt[:, 2 * P:4 * P].rearrange("p (c k) -> p c k", k=P)).then_inc(s_trk, 1)
                    dve.wait_ge(s_trk, t + 1)
                    for a in range(2):
                        dve.wait_ge(s_dx, 4 * t + 2 * a + 2)
                        decays = ex[:, p, a, 0:NL * P].rearrange("p (l k) -> p l k", k=P)
                        dve.tensor_tensor(kx[:, p, a], decays, qkT[:, p, 2 + a:3 + a].to_broadcast([P, NL, P]), ALU.mult).then_inc(s_kx, 1)
                        dve.tensor_tensor(qx[:, p, a], decays, qkT[:, p, a:a + 1].to_broadcast([P, NL, P]), ALU.mult).then_inc(s_qx, 1)
                        dve.tensor_tensor(qb[:, p, a].rearrange("p (c x) -> p c x", x=3 * CHUNK)[:, :, 0:CHUNK],
                                          ex[:, p, a, NL * P:DCOLS].rearrange("p (c x) -> p c x", x=CHUNK),
                                          qkT[:, p, a].rearrange("p (c x) -> p c x", x=CHUNK), ALU.mult).then_inc(s_qb, 1)
                    dve.wait_ge(s_nx, t + 1)
                    dve.wait_ge(s_in[p], 48 * (h + 1))
                    dve.tensor_tensor(ke[:, p], qk[:, p, 256:512], ken[:, p], ALU.mult).then_inc(s_ke, 1)

            pipeline(dve, slot)

        @block.gpsimd
        def _(pool):
            pool.memset(half_pow[:], -0.5).then_inc(s_cs, 1)
            pool.wait_ge(s_cs, 1)
            pool.wait_ge(s_c, 128)

            def slot(h, p, stages, sample):
                if 1 in stages:
                    t = h * 2 + p
                    if 3 in stages:
                        pool.wait_ge(s_n, t - 1)
                    stop_at(pool, s_in[p], 48 * (h + 1), s_pass_pool)
                    pool.tensor_copy(lah[:, p], lat[:, p]).then_inc(s_lh, 1)
                    pool.wait_ge(s_lh, t + 1)
                    pool.tensor_tensor(lal[:, p], lat[:, p], raw(lah[:, p]), ALU.subtract).then_inc(s_ll, 1)
                if 3 in stages:
                    h2, p2, t2 = before(h, p, 2)
                    stop_at(pool, s_ss, t2 + 1, s_pass_pool)
                    pool.tensor_scalar(ms4[:], ss4[:], 1.0 / DV, EPS, ALU.mult, ALU.add).then_inc(s_ms, 1)
                    pool.wait_ge(s_ms, t2 + 1)
                    pool.wait_ge(s_on, t2)
                    pool.tensor_tensor(r4[:], ms4[:], half_pow[:], ALU.pow).then_inc(s_r, 1)
                if 3 in stages:
                    pool.wait_ge(s_on, t2 + 1)
                    pool.wait_ge(s_md[p2], 16 * h2)
                    pool.tensor_tensor(mo[:, p2], on[:], sgg[:, p2], ALU.mult).then_inc(s_mo, 1)
                if 2 in stages:
                    h1, p1, t = before(h, p, 1)
                    pool.wait_ge(s_in[p1], 48 * (h1 + 1))
                    if 3 in stages:
                        pool.wait_ge(s_mo, t - 1)
                    pool.tensor_tensor(sgg[:, p1], sg[:, p1], gb[:].rearrange("p h d -> p (h d)"), ALU.mult).then_inc(s_sgg, 1)

            pipeline(pool, slot)


def attention_operands(m):
    kt = m.sb("kt", [P, 2, KEYS], F32R)
    qh = m.sb("qh", [P, 2, ROWS], F32R)
    ql = m.sb("ql", [P, 2, ROWS], F32R)
    v = m.sb("v", [P, 2, KEYS // P, HD])
    return kt, qh, ql, v


def load_head(sp, operands, h, p, qT, kT, new_v, cache_v, s_in, s_v):
    kt, qh, ql, v = operands

    def head(ap):
        return ap[bass.ds(h, 1)].rearrange("o p k -> p (o k)")

    sp.dma_start(raw(kt[:, p]), head(kT)).then_inc(s_in, 16)
    for half in range(2):
        ps = slice(64 * half, 64 * half + 64)
        sp.dma_start(raw(qh[ps, p]), head(qT)[0:64]).then_inc(s_in, 16)
        sp.dma_start(raw(ql[ps, p]), head(qT)[64:128]).then_inc(s_in, 16)
    cols = bass.ds(h * HD, HD)
    sp.dma_start(v[:, p, 0:SEQ // P], new_v[0:SEQ, cols].rearrange("(t p) c -> p t c", p=P)).then_inc(s_v, 16)
    sp.dma_start(v[:, p, SEQ // P:NEW_KEY_COL // P], cache_v[:, cols].rearrange("(t p) c -> p t c", p=P)).then_inc(s_v, 16)
    sp.dma_start(v[0:DEC, p, NEW_KEY_COL // P], new_v[SEQ:SEQ + DEC, cols]).then_inc(s_v, 16)


def attention_units():
    units = []
    for t in range(TILES):
        lo, n = (0, t + 1) if t < TILES - 1 else (SEQ // P, PAST // P + 1)
        if n <= 8:
            units.append((t, lo, n, True, True))
        else:
            low = n // 2
            units.append((t, lo + low, n - low, True, False))
            units.append((t, lo, low, False, True))
    return units


def phase_attention(nc, operands, qT, kT, new_v, cache_v, ident, diag_mask, mix, w_out, wh, wl):
    units = [(p, *u) for p in range(2) for u in attention_units()]
    NU = len(units)
    LEAD = 4
    units += units[:LEAD + 2]
    groups = [[(g, min(4, n - 4 * g)) for g in range((n + 3) // 4)] for _, _, _, n, _, _ in units]
    first_group = [sum(len(g) for g in groups[:u]) for u in range(len(units) + 1)]
    NGR = first_group[NU]
    tiles_done = [sum(x[5] for x in units[:u]) for u in range(len(units) + 1)]
    NT = 2 * TILES
    with Pool(nc, "sb") as m:
        idt = m.sb("idt", [P, P])
        idr = m.sb("idr", [P, P], F32R)
        dm = m.sb("dm", [P, P])
        dmr = m.sb("dmr", [P, P], F32R)
        kt, qh, ql, v = operands
        a = m.sb("a", [P, 3, 1024])
        g = m.sb("g", [P, 2, 1024])
        w = m.sb("w", [P, 2, 1024])
        ssum = m.sb("ssum", [P, 1])
        wt = m.sb("wt", [P, 4, 512])
        os_ = m.sb("os", [P, 2, TILES, HD])
        wr = m.sb("wr", [P, 2, 2, 512])
        z = m.ps("z", [P, 2, 1024])
        tp = m.ps("tp", [P, 2, 512])
        po = m.ps("po", [P, 2, 512])
        names = ("c", "cr", "z", "ab", "ex", "ln", "sp", "ss", "gt", "sc", "w", "tr", "wt", "pv", "of")
        s_c, s_cr, s_z, s_ab, s_ex, s_ln, s_sp, s_ss, s_gt, s_sc, s_w, s_tr, s_wt, s_pv, s_of = [m.sem(n) for n in names]
        s_wr, s_wh, s_wl = m.sems("wr", 2), m.sem("wh"), m.sem("wl")
        pieces = [(n, c) for n in range(2) for c in range(0, KC, 2)]
        s_in, s_v, s_os = m.sems("in", 2), m.sems("v", 2), m.sems("os", 2)
        block = m.block()

        def place(u, ring, turn=NU):
            return u % turn % ring

        def last_in(u, ring, turn=NU):
            v = u - 1
            while place(v, ring, turn) != place(u, ring, turn):
                v -= 1
            return max(v + 1, 0)

        def turns(eng, slot):
            def unit(s, last):
                return lambda k: s - k if 0 <= s - k and not (last and s - k >= NU) else None

            for s in range(LEAD):
                slot(0, s, unit(s, False))
            with eng.Fori(0, SB_HEADS // 2 - 1) as i:
                for s in range(LEAD, NU + LEAD):
                    slot(i, s, unit(s, False))
            for s in range(LEAD, NU + LEAD):
                slot(SB_HEADS // 2 - 1, s, unit(s, True))

        @block.sync
        def _(sp):
            sp.dma_start(idt[:], ident).then_inc(s_c, 16)
            sp.dma_start(dm[:], diag_mask).then_inc(s_c, 16)

            def load(h, p):
                load_head(sp, operands, h, p, qT, kT, new_v, cache_v, s_in[p], s_v[p])

            def turn(i, last):
                for p in range(2):
                    if p == 0 or not last:
                        sp.wait_ge(s_pv, i * NGR + first_group[p * NU // 2])
                        load(2 * i + 1 + p, 1 - p)
                    sp.wait_ge(s_of, i * NT + (p + 1) * TILES)
                    sp.dma_start(mix[:, bass.ds((2 * i + p) * HD + 512, HD)].rearrange("(t p) c -> p t c", p=P),
                                 os_[:, p]).then_inc(s_os[p], 16)

            for k, (n, c) in enumerate(pieces):
                if k >= 2:
                    sp.wait_ge(s_wl, k - 1)
                sp.dma_start(wr[:, k % 2], w_out[c * P:(c + 2) * P, n * 512:(n + 1) * 512]
                             .rearrange("(c p) n -> p c n", p=P)).then_inc(s_wr[k % 2], 16)
            with sp.Fori(0, SB_HEADS // 2 - 1) as i:
                turn(i, False)
            turn(SB_HEADS // 2 - 1, True)
            for p in range(2):
                sp.wait_ge(s_os[p], 16 * SB_HEADS // 2)

        @block.gpsimd
        def _(pool):
            for k, (n, c) in enumerate(pieces):
                pool.wait_ge(s_wr[k % 2], 16 * (k // 2 + 1))
                pool.tensor_copy(wh[:, n, c:c + 2], wr[:, k % 2]).then_inc(s_wh, 1)
                pool.wait_ge(s_wh, k + 1)
                pool.tensor_tensor(wl[:, n, c:c + 2], wr[:, k % 2], raw(wh[:, n, c:c + 2]), ALU.subtract).then_inc(s_wl, 1)

        @block.tensor
        def _(pe):
            pe.wait_ge(s_cr, 2)

            def logits(i, u):
                p, t, lo, n, first, last = units[u]
                if u % (NU // 2) == 0:
                    if p == 1 or u > 0:
                        pe.wait_ge(s_in[p], 80 * (i + (u // NU + p)))
                pe.wait_ge(s_sc, i * NU + max(u - 1, 0))
                for b in range((n + 3) // 4):
                    nb = min(4, n - 4 * b)
                    dst = z[:, u % 2, 512 * b:512 * b + nb * P]
                    keys = kt[:, p, (lo + 4 * b) * P:(lo + 4 * b + nb) * P]
                    masked = first and 4 * b + nb == n
                    pe.matmul(dst, qh[:, p, t * P:(t + 1) * P], keys, start=True, stop=False)
                    mm = pe.matmul(dst, ql[:, p, t * P:(t + 1) * P], keys, start=False, stop=not masked)
                    if masked:
                        mm = pe.matmul(z[:, u % 2, (n - 1) * P:n * P], idr[:], dmr[:], start=False, stop=True)
                mm.then_inc(s_z, 1)

            def transposes(i, u, j):
                if j < len(groups[u]):
                    g4, nb = groups[u][j]
                    gi = first_group[u] + j
                    pe.wait_ge(s_w, i * NU + u + 1)
                    pe.wait_ge(s_wt, i * NGR + max(gi - 1, 0))
                    for c in range(nb):
                        mm = pe.transpose(tp[:, gi % 2, c * P:(c + 1) * P], w[:, u % 2, (4 * g4 + c) * P:(4 * g4 + c + 1) * P], idt[:])
                    mm.then_inc(s_tr, 1)

            def values(i, u):
                p, t, lo, n, first, last = units[u]
                tt = tiles_done[u]
                if u % (NU // 2) == 0:
                    if p == 1 or u > 0:
                        pe.wait_ge(s_v[p], 48 * (i + (u // NU + p)))
                if first:
                    pe.wait_ge(s_of, i * NT + max(tt - 1, 0))
                for j, (g4, nb) in enumerate(groups[u]):
                    gi = first_group[u] + j
                    pe.wait_ge(s_wt, i * NGR + gi + 1)
                    for c in range(nb):
                        key = lo + 4 * g4 + c
                        mm = pe.matmul(po[:, tt % 2, 0:HD], wt[:, place(gi, 4, NGR), c * P:(c + 1) * P], v[:, p, key],
                                       start=(first and j == 0 and c == 0), stop=(last and 4 * g4 + c == n - 1))
                    mm.then_inc(s_pv, 1)

            def slot(i, s, u):
                if u(2) is not None:
                    transposes(i, u(2), 0)
                if u(2) is not None:
                    transposes(i, u(2), 1)
                if u(-1) is not None:
                    logits(i, u(-1))
                if u(3) is not None:
                    values(i, u(3))

            logits(0, 0)
            turns(pe, slot)

        @block.scalar
        def _(act):
            act.preload_act_table_set("natural_log_exp_and_others")
            act.wait_ge(s_c, 32)
            act.activation(idr[:], idt[:], ACT.Copy).then_inc(s_cr, 1)
            act.activation(dmr[:], dm[:], ACT.Copy).then_inc(s_cr, 1)

            def absolute(i, u):
                act.wait_ge(s_z, i * NU + u + 1)
                act.wait_ge(s_sc, i * NU + last_in(u, 3))
                n = units[u][3] * P
                act.activation(a[:, place(u, 3), 0:n], z[:, u % 2, 0:n], ACT.Abs).then_inc(s_ab, 1)

            def weights(i, u):
                act.wait_ge(s_sc, i * NU + u + 1)
                act.wait_ge(s_tr, i * NGR + first_group[max(u - 1, 0)])
                n = units[u][3] * P
                act.activation(w[:, u % 2, 0:n], g[:, u % 2, 0:n], ACT.Exp, scale=-1.0).then_inc(s_w, 1)

            def exponential(i, u):
                act.wait_ge(s_ab, i * NU + u + 1)
                n = units[u][3] * P
                act.activation(a[:, place(u, 3), 0:n], a[:, place(u, 3), 0:n], ACT.Exp, scale=-1.0).then_inc(s_ex, 1)

            def logarithm(i, u):
                act.wait_ge(s_ex, i * NU + u + 1)
                n = units[u][3] * P
                act.activation(a[:, place(u, 3), 0:n], a[:, place(u, 3), 0:n], ACT.Ln, bias=1.0).then_inc(s_ln, 1)

            def slot(i, s, u):
                if u(0) is not None:
                    exponential(i, u(0))
                    logarithm(i, u(0))
                if u(1) is not None:
                    weights(i, u(1))
                if u(-1) is not None:
                    absolute(i, u(-1))

            absolute(0, 0)
            turns(act, slot)

        @block.vector
        def _(dve):
            followed = [not x[5] for x in units]
            nf = [sum(followed[:u]) for u in range(len(units) + 1)]

            def negated_softplus(i, u):
                n = units[u][3] * P
                dve.wait_ge(s_ln, i * NU + u + 1)
                dve.scalar_tensor_tensor(out=a[:, place(u, 3), 0:n], in0=z[:, u % 2, 0:n], scalar=0.0, in1=a[:, place(u, 3), 0:n],
                                         op0=ALU.min, op1=ALU.subtract).then_inc(s_sp, 1)
                dve.wait_ge(s_w, i * NU + last_in(u, 2))
                top = g[:, u % 2, n - 1:n]
                if units[u][4]:
                    dve.memset(top, -NEG).then_inc(s_gt, 1)
                else:
                    dve.wait_ge(s_sp, i * NU + u + 1)
                    dve.wait_ge(s_sc, i * NU + u)
                    dve.tensor_tensor(top, ssum[:], a[:, place(u, 3), n - 1:n], ALU.subtract).then_inc(s_gt, 1)

            def scan(i, u):
                n = units[u][3] * P
                dve.wait_ge(s_sp, i * NU + u + 1)
                dve.wait_ge(s_gt, i * NU + u + 1)
                ins = dve.tensor_tensor_scan(g[:, u % 2, n - 2::-1], z[:, u % 2, n - 1:0:-1], a[:, place(u, 3), n - 2::-1],
                                             g[:, u % 2, n - 1:n], ALU.add, ALU.subtract)
                if followed[u]:
                    ins.then_inc(s_ss, 1)
                    dve.wait_ge(s_ss, i * nf[NU] + nf[u] + 1)
                    ins = dve.tensor_tensor(ssum[:], g[:, u % 2, 0:1], z[:, u % 2, 0:1], ALU.add)
                ins.then_inc(s_sc, 1)

            def transposed(i, u, j):
                if j < len(groups[u]):
                    nb = groups[u][j][1]
                    gi = first_group[u] + j
                    dve.wait_ge(s_tr, i * NGR + gi + 1)
                    dve.wait_ge(s_pv, i * NGR + last_in(gi, 4, NGR))
                    dve.tensor_copy(wt[:, place(gi, 4, NGR), 0:nb * P], tp[:, gi % 2, 0:nb * P]).then_inc(s_wt, 1)

            def output(i, u):
                p, t, lo, n, first, last = units[u]
                if last:
                    tt = tiles_done[u]
                    dve.wait_ge(s_pv, i * NGR + first_group[u + 1])
                    if tt % TILES == 0:
                        dve.wait_ge(s_os[p], 16 * (i + u // NU))
                    dve.tensor_copy(os_[:, p, t, :], po[:, tt % 2, 0:HD]).then_inc(s_of, 1)

            def slot(i, s, u):
                if u(4) is not None:
                    output(i, u(4))
                if u(2) is not None:
                    transposed(i, u(2), 0)
                if u(0) is not None:
                    negated_softplus(i, u(0))
                if u(2) is not None:
                    transposed(i, u(2), 1)
                if u(0) is not None:
                    scan(i, u(0))

            turns(dve, slot)


def phase_output(nc, mix, x, wh, wl, norm_g, ident, h_out, hTh, hTl):
    with Pool(nc, "ot") as m:
        idt = m.sb("idt", [P, P])
        gb = m.sb("gb", [P, D])
        half_pow = m.sb("half_pow", [P, 1])
        mi = m.sb("mi", [P, 2, D])
        xb = m.sb("xb", [P, 2, D])
        mh = m.sb("mh", [P, 2, KC, P], F32R)
        ml = m.sb("ml", [P, 2, KC, P], F32R)
        hb = m.sb("hb", [P, 2, D])
        hn = m.sb("hn", [P, 2, D])
        ss = m.sb("ss", [P, 2, 3])
        sh = m.sb("sh", [P, 2, KC, P], F32R)
        sl = m.sb("sl", [P, 2, KC, P], F32R)
        ta = m.ps("ta", [P, D])
        tb = m.ps("tb", [P, D])
        pp = m.ps("pp", [P, 2, D])
        names = ("c", "cs", "a", "mh", "ml", "b", "h", "sq", "ms", "r", "hn", "t", "sh", "sl")
        s_c, s_cs, s_a, s_mh, s_ml, s_b, s_h, s_sq, s_ms, s_r, s_hn, s_t, s_sh, s_sl = [m.sem(n) for n in names]
        s_pass_sp, s_pass_pool = m.sem("pass_sp"), m.sem("pass_pool")
        s_m, s_x, s_ho, s_ho2 = m.sems("m", 2), m.sems("x", 2), m.sems("ho", 2), m.sems("ho2", 2)
        block = m.block()

        def pipeline(eng, slot):
            slot(0, 0, "A")
            slot(0, 1, "AB")
            with eng.Fori(0, (TILES - 3) // 2) as i:
                slot(i + 1, 0, "ABC")
                slot(i + 1, 1, "ABC")
            slot((TILES - 1) // 2, 0, "ABC")
            slot((TILES - 1) // 2, 1, "BC")
            slot((TILES + 1) // 2, 0, "C")

        def before(k, p, n):
            q = p - n
            k = k + q // 2
            return k, q % 2, k * 2 + q % 2

        @block.sync
        def _(sp):
            sp.dma_start(idt[:], ident).then_inc(s_c, 16)
            sp.dma_start(gb[:], bcast_rows(norm_g, D)).then_inc(s_c, 16)
            sp.dma_start(mi[:, 0], rows(mix, 0)).then_inc(s_m[0], 16)
            sp.dma_start(xb[:, 0], rows(x, 0)).then_inc(s_x[0], 16)
            sp.dma_start(mi[:, 1], rows(mix, 1)).then_inc(s_m[1], 16)
            sp.dma_start(xb[:, 1], rows(x, 1)).then_inc(s_x[1], 16)

            def slot(k, p, stages):
                t = k * 2 + p
                if "A" in stages and "B" in stages and not (isinstance(k, int) and t == TILES - 1):
                    _, p1, t1 = before(k, p, -1)
                    sp.wait_ge(s_a, t)
                    sp.dma_start(mi[:, p1], rows(mix, t1)).then_inc(s_m[p1], 16)
                if "B" in stages:
                    _, p1, t1 = before(k, p, 1)
                    sp.wait_ge(s_h, t1 + 1)
                    sp.dma_start(rows(h_out, t1), hb[:, p1]).then_inc(s_ho[p1], 16)
                    if "A" in stages and not (isinstance(k, int) and t == TILES - 1):
                        _, p2, t2 = before(k, p, -1)
                        sp.dma_start(xb[:, p2], rows(x, t2)).then_inc(s_x[p2], 16)
                if "C" in stages:
                    _, p2, t2 = before(k, p, 2)
                    stop_at(sp, s_sl, t2 + 1, s_pass_sp)
                    for dst, src in ((hTh, sh), (hTl, sl)):
                        sp.dma_start(dst[:, :, bass.ds(t2 * P, P)].rearrange("c k t -> k c t"), raw(src[:, p2])).then_inc(s_ho2[p2], 16)

            pipeline(sp, slot)
            for p in range(2):
                n = (TILES + 1 - p) // 2
                sp.wait_ge(s_ho[p], 16 * n)
                sp.wait_ge(s_ho2[p], 32 * n)

        @block.tensor
        def _(pe):
            pe.wait_ge(s_c, 32)

            def slot(k, p, stages):
                if "A" in stages:
                    t = k * 2 + p
                    pe.wait_ge(s_m[p], 16 * (k + 1))
                    pe.wait_ge(s_ml, t)
                    for c in range(KC):
                        mm = pe.transpose(ta[:, c * P:(c + 1) * P], mi[:, p, c * P:(c + 1) * P], idt[:])
                    mm.then_inc(s_a, 1)
                if "B" in stages:
                    k1, p1, t = before(k, p, 1)
                    pe.wait_ge(s_ml, t + 1)
                    if not isinstance(t, int) or t >= 2:
                        pe.wait_ge(s_h, t - 1)
                    for n in range(2):
                        for i, (mm_, ww) in enumerate(((mh, wh), (mh, wl), (ml, wh))):
                            for c in range(KC):
                                mm = pe.matmul(pp[:, p1, n * 512:(n + 1) * 512], mm_[:, p1, c], ww[:, n, c],
                                               start=(i == 0 and c == 0), stop=(i == 2 and c == KC - 1))
                    mm.then_inc(s_b, 1)
                if "C" in stages:
                    k2, p2, t = before(k, p, 2)
                    pe.wait_ge(s_hn, t + 1)
                    pe.wait_ge(s_sl, t)
                    for c in range(KC):
                        mm = pe.transpose(tb[:, c * P:(c + 1) * P], hn[:, p2, c * P:(c + 1) * P], idt[:])
                    mm.then_inc(s_t, 1)

            pipeline(pe, slot)

        @block.scalar
        def _(act):
            act.preload_act_table_set("natural_log_exp_and_others")

            def slot(k, p, stages):
                if "A" in stages:
                    t = k * 2 + p
                    act.wait_ge(s_a, t + 1)
                    if "C" in stages:
                        act.wait_ge(s_b, t - 1)
                    act.activation(mh[:, p], ta[:].rearrange("p (c k) -> p c k", k=P), ACT.Copy).then_inc(s_mh, 1)
                if "C" in stages:
                    k2, p2, t = before(k, p, 2)
                    act.wait_ge(s_t, t + 1)
                    act.wait_ge(s_ho2[p2], 32 * k2)
                    act.activation(sh[:, p2], tb[:].rearrange("p (c k) -> p c k", k=P), ACT.Copy).then_inc(s_sh, 1)
                if "B" in stages:
                    k1, p1, t = before(k, p, 1)
                    act.wait_ge(s_h, t + 1)
                    if not isinstance(t, int) or t >= 2:
                        act.wait_ge(s_t, t - 1)
                    act.activation(hn[:, p1], hb[:, p1], ACT.Square, accum_out=ss[:, p1, 0:1]).then_inc(s_sq, 1)

            pipeline(act, slot)

        @block.vector
        def _(dve):
            dve.wait_ge(s_c, 32)

            def slot(k, p, stages):
                if "A" in stages:
                    t = k * 2 + p
                    dve.wait_ge(s_mh, t + 1)
                    dve.tensor_tensor(ml[:, p], ta[:].rearrange("p (c k) -> p c k", k=P), raw(mh[:, p]), ALU.subtract).then_inc(s_ml, 1)
                if "C" in stages:
                    k2, p2, t = before(k, p, 2)
                    dve.wait_ge(s_sh, t + 1)
                    dve.tensor_tensor(sl[:, p2], tb[:].rearrange("p (c k) -> p c k", k=P), raw(sh[:, p2]), ALU.subtract).then_inc(s_sl, 1)
                if "B" in stages:
                    k1, p1, t = before(k, p, 1)
                    dve.wait_ge(s_b, t + 1)
                    dve.wait_ge(s_x[p1], 16 * (k1 + 1))
                    dve.wait_ge(s_ho[p1], 16 * k1)
                    dve.tensor_tensor(hb[:, p1], pp[:, p1], xb[:, p1], ALU.add).then_inc(s_h, 1)
                    dve.wait_ge(s_r, t + 1)
                    dve.scalar_tensor_tensor(out=hn[:, p1], in0=hb[:, p1], scalar=ss[:, p1, 2:3], in1=gb[:],
                                             op0=ALU.mult, op1=ALU.mult).then_inc(s_hn, 1)

            pipeline(dve, slot)

        @block.gpsimd
        def _(pool):
            pool.memset(half_pow[:], -0.5).then_inc(s_cs, 1)
            pool.wait_ge(s_cs, 1)

            def slot(k, p, stages):
                if "B" in stages:
                    k1, p1, t = before(k, p, 1)
                    stop_at(pool, s_sq, t + 1, s_pass_pool)
                    pool.tensor_scalar(ss[:, p1, 1:2], ss[:, p1, 0:1], 1.0 / D, EPS, ALU.mult, ALU.add).then_inc(s_ms, 1)
                    pool.wait_ge(s_ms, t + 1)
                    pool.tensor_tensor(ss[:, p1, 2:3], ss[:, p1, 1:2], half_pow[:], ALU.pow).then_inc(s_r, 1)

            pipeline(pool, slot)


FG = 256
FC = FG // P
NFG = D_FF // FG


def phase_mlp(nc, hTh, hTl, h, w_up, w_down, y):
    NB = FULL_BLOCKS + 1
    nts = [BT] * FULL_BLOCKS + [LAST_BT]
    tokens = [BT * P] * FULL_BLOCKS + [BT * P + DEC]
    W = LAST_BT * P
    with Pool(nc, "ml") as m:
        xh = m.sb("xh", [P, 2, KC, W], F32R)
        xl = m.sb("xl", [P, 2, KC, W], F32R)
        ya = m.sb("ya", [P, LAST_BT, D])
        ur = m.sb("ur", [P, KC, FG])
        uh = m.sb("uh", [P, 2, KC, FG], F32R)
        ul = m.sb("ul", [P, 2, KC, FG], F32R)
        dr = m.sb("dr", [P, FC, D])
        dh = m.sb("dh", [P, 2, FC, D], F32R)
        dl = m.sb("dl", [P, 2, FC, D], F32R)
        r = m.sb("r", [P, FC, W])
        th = m.sb("th", [P, 2, FC, W], F32R)
        tl = m.sb("tl", [P, 2, FC, W], F32R)
        pu = m.ps("pu", [P, FC, 2, 512])
        pd = m.ps("pd", [P, 2, D])
        names = ("ur", "dr", "uh", "ul", "dh", "dl", "up", "r", "sq", "th", "tl", "dn", "ya")
        s_ur, s_dr, s_uh, s_ul, s_dh, s_dl, s_up, s_r, s_sq, s_th, s_tl, s_dn, s_ya = [m.sem(n) for n in names]
        s_hx, s_lx = m.sems("hx", 2), m.sems("lx", 2)
        s_ul0, s_pad = m.sem("ul0"), m.sem("pad")
        s_y, s_yo = m.sems("y", LAST_BT), m.sems("yo", LAST_BT)
        block = m.block()
        CRED = LAST_BT

        def steps(eng, step, enter=lambda b: None, leave=lambda b: None):
            for b in range(NB):
                enter(b)
                with eng.Fori(0, NFG // 2 - 2) as i:
                    step(b, 2 * i, 0)
                    step(b, 2 * i + 1, 1)
                for g in range(NFG - 4, NFG):
                    step(b, g, g % 2)
                leave(b)

        def ahead(b, g, n):
            if isinstance(g, int):
                b, g = b + (g + n) // NFG, (g + n) % NFG
                return (b, g) if b < NB else None
            return b, g + n

        def number(b, g):
            return g + b * NFG

        def tile_no(b, g, j):
            return g * nts[b] + (b * NFG * BT + j)

        @block.sync
        def _(sp):
            def load_up(b, g):
                sp.wait_ge(s_ul, number(b, g))
                sp.dma_start(ur[:], w_up[:, bass.ds(g * FG, FG)].rearrange("(c p) n -> p c n", p=P)).then_inc(s_ur, 16)

            def load_down(b, g):
                sp.wait_ge(s_dl, number(b, g))
                sp.dma_start(dr[:], w_down[bass.ds(g * FG, FG), :].rearrange("(c p) n -> p c n", p=P)).then_inc(s_dr, 16)

            def load_rows(b):
                n = tokens[b]
                for dst, src, sem in ((xh, hTh, s_hx), (xl, hTl, s_lx)):
                    sp.dma_start(raw(dst[:, b % 2, :, 0:n]), src[:, :, b * BT * P:b * BT * P + n].rearrange("c k t -> k c t")).then_inc(sem[b % 2], 16)

            def load_y(b, j):
                sp.dma_start(ya[:, j], rows(h, b * BT + j)).then_inc(s_y[j], 16)

            sp.dma_start(ur[:], w_up[:, 0:FG].rearrange("(c p) n -> p c n", p=P)).then_inc(s_ur, 16)
            load_rows(0)
            load_up(0, 1)
            load_down(0, 0)
            for j in range(nts[0]):
                load_y(0, j)
            load_up(0, 2)
            load_down(0, 1)

            def enter(b):
                if b + 1 < NB:
                    sp.wait_ge(s_up, b * NFG * FC)
                    load_rows(b + 1)

            def step(b, g, p):
                n = ahead(b, g, 3)
                if n:
                    load_up(*n)
                n = ahead(b, g, 2)
                if n:
                    load_down(*n)

            def leave(b):
                for j in range(nts[b]):
                    t = b * BT + j
                    sp.wait_ge(s_ya, tile_no(b, NFG - 1, j) + 1 + CRED)
                    n = DEC if t == TILES - 1 else P
                    sp.dma_start(y[t * P:t * P + n, :], ya[0:n, j]).then_inc(s_yo[j], 16)
                if b + 1 < NB:
                    for j in range(nts[b + 1]):
                        if j < nts[b]:
                            sp.wait_ge(s_yo[j], 16 * (b + 1))
                        load_y(b + 1, j)

            steps(sp, step, enter, leave)
            for j in range(LAST_BT):
                sp.wait_ge(s_yo[j], 16 * (NB if j < BT else 1))

        @block.tensor
        def _(pe):
            def up(b, g, p):
                G = number(b, g)
                n = tokens[b]
                cuts = [(0, 0, n)] if n <= 512 else [(0, 0, n // 2), (1, n // 2, n // 2)]
                pe.wait_ge(s_ul, G + 1)
                pe.wait_ge(s_r, G * FC)
                for f in range(FC):
                    for i, (w, xx) in enumerate(((uh, xh), (uh, xl), (ul, xh))):
                        for c in range(KC):
                            if isinstance(g, int) and g == 0 and f == 0 and i == 1 and c == 0:
                                pe.wait_ge(s_lx[b % 2], 16 * (b // 2 + 1))
                            for bank, at, size in cuts:
                                mm = pe.matmul(pu[:, f, bank, 0:size], w[:, p, c, f * P:(f + 1) * P], xx[:, b % 2, c, at:at + size],
                                               start=(i == 0 and c == 0), stop=(i == 2 and c == KC - 1))
                    mm.then_inc(s_up, 1)

            def down(b, g, p):
                G = number(b, g)
                pe.wait_ge(s_dl, G + 1)
                pe.wait_ge(s_tl, (G + 1) * FC)
                for j in range(nts[b]):
                    pe.wait_ge(s_ya, tile_no(b, g, j) - 1 + CRED)
                    q = (p * nts[b] + j) % 2
                    for n in range(2):
                        for i, (tt, w) in enumerate(((th, dh), (th, dl), (tl, dh))):
                            for f in range(FC):
                                mm = pe.matmul(pd[:, q, n * 512:(n + 1) * 512], tt[:, p, f, j * P:(j + 1) * P],
                                               w[:, p, f, n * 512:(n + 1) * 512],
                                               start=(i == 0 and f == 0), stop=(i == 2 and f == FC - 1))
                    mm.then_inc(s_dn, 1)

            pe.wait_ge(s_hx[0], 16)
            up(0, 0, 0)
            pe.wait_ge(s_pad, 2)

            def step(b, g, p):
                n = ahead(b, g, 1)
                if n:
                    if n[0] != b:
                        pe.wait_ge(s_hx[n[0] % 2], 16 * (n[0] // 2 + 1))
                    up(*n, 1 - p)
                down(b, g, p)

            steps(pe, step)

        @block.scalar
        def _(act):
            act.preload_act_table_set("natural_log_exp_and_others")

            def split_up(b, g, p):
                G = number(b, g)
                act.wait_ge(s_ur, (G + 1) * 16)
                if not (isinstance(g, int) and b == 0 and g < 2):
                    act.wait_ge(s_up, (G - 1) * FC)
                act.activation(uh[:, p], ur[:], ACT.Copy).then_inc(s_uh, 1)

            def split_down(b, g, p):
                G = number(b, g)
                act.wait_ge(s_dr, (G + 1) * 16)
                if not (isinstance(g, int) and b == 0 and g == 0):
                    before_last(act, b, g)
                act.activation(dh[:, p], dr[:], ACT.Copy).then_inc(s_dh, 1)

            def before_last(eng, b, g):
                if isinstance(g, int) and g < 1:
                    eng.wait_ge(s_dn, tile_no(b - 1, NFG - 1, 0))
                else:
                    eng.wait_ge(s_dn, tile_no(b, g - 1, 0))

            def hidden(b, g, p):
                G = number(b, g)
                n = tokens[b]
                for f in range(FC):
                    src = pu[:, f, 0, 0:n] if n <= 512 else pu[:, f, :, 0:n // 2]
                    dst = r[:, f, 0:n] if n <= 512 else r[:, f, 0:n].rearrange("p (a k) -> p a k", a=2)
                    act.wait_ge(s_up, G * FC + f + 1)
                    act.wait_ge(s_tl, G * FC)
                    act.activation(dst, src, ACT.Relu).then_inc(s_r, 1)
                for f in range(FC):
                    act.wait_ge(s_r, G * FC + f + 1)
                    if not (isinstance(g, int) and b == 0 and g < 2):
                        if f == 0:
                            before_last(act, b, g)
                    act.activation(th[:, p, f, 0:n], r[:, f, 0:n], ACT.Square).then_inc(s_th, 1)

            split_up(0, 0, 0)
            split_up(0, 1, 1)
            split_down(0, 0, 0)
            hidden(0, 0, 0)

            def step(b, g, p):
                n = ahead(b, g, 2)
                if n:
                    split_up(*n, p)
                n = ahead(b, g, 1)
                if n:
                    split_down(*n, 1 - p)
                    hidden(*n, 1 - p)

            steps(act, step)

        @block.gpsimd
        def _(pool):
            def split_up(b, g, p):
                pool.wait_ge(s_uh, number(b, g) + 1)
                pool.tensor_tensor(ul[:, p], ur[:], raw(uh[:, p]), ALU.subtract).then_inc(s_ul, 1)

            pool.wait_ge(s_ul0, 1)
            pool.sem_inc(s_ul, 1)
            split_up(0, 1, 1)

            def step(b, g, p):
                n = ahead(b, g, 2)
                if n:
                    split_up(*n, p)

            steps(pool, step)

        @block.vector
        def _(dve):
            dve.sem_inc(s_ya, CRED)
            dve.memset(raw(th[:, :, :, tokens[-1]:W]), 0.0).then_inc(s_pad, 1)
            dve.memset(raw(tl[:, :, :, tokens[-1]:W]), 0.0).then_inc(s_pad, 1)
            dve.wait_ge(s_uh, 1)
            dve.tensor_tensor(ul[:, 0], ur[:], raw(uh[:, 0]), ALU.subtract).then_inc(s_ul0, 1)

            def split_down(b, g, p):
                dve.wait_ge(s_dh, number(b, g) + 1)
                dve.tensor_tensor(dl[:, p], dr[:], raw(dh[:, p]), ALU.subtract).then_inc(s_dl, 1)

            def hidden(b, g, p):
                G = number(b, g)
                n = tokens[b]
                for f in range(FC):
                    dve.wait_ge(s_th, G * FC + f + 1)
                    dve.tensor_tensor(r[:, f, 0:n], r[:, f, 0:n], r[:, f, 0:n], ALU.mult).then_inc(s_sq, 1)
                for f in range(FC):
                    dve.wait_ge(s_sq, G * FC + f + 1)
                    dve.tensor_tensor(tl[:, p, f, 0:n], r[:, f, 0:n], raw(th[:, p, f, 0:n]), ALU.subtract).then_inc(s_tl, 1)

            def add(b, g, p):
                for j in range(nts[b]):
                    k = tile_no(b, g, j)
                    dve.wait_ge(s_dn, k + 1)
                    dve.wait_ge(s_y[j], 16 * (b + 1) if j < BT else 16)
                    dve.wait_ge(s_ya, k - nts[b] + 1 + CRED)
                    q = (p * nts[b] + j) % 2
                    dve.tensor_tensor(ya[:, j], ya[:, j], pd[:, q], ALU.add).then_inc(s_ya, 1)

            split_down(0, 0, 0)
            hidden(0, 0, 0)

            def step(b, g, p):
                n = ahead(b, g, 1)
                if n:
                    split_down(*n, 1 - p)
                    hidden(*n, 1 - p)
                add(b, g, p)

            steps(dve, step)


def gla_constants(np):
    j, t = np.arange(P)[:, None], np.arange(P)[None, :]
    same = j // CHUNK == t // CHUNK
    cols, masks = [], []
    for half in LEVELS:
        block = t // (2 * half) * (2 * half)
        mid = block + half
        is_right = t >= mid
        cols.append(np.where(is_right, (j >= mid) & (j <= t), (j > t) & (j < mid)))
        rights = np.arange(P)[(np.arange(P) // half) % 2 == 1][None, :]
        masks.append((j // (2 * half) == rights // (2 * half)) & ((j // half) % 2 == 0))
    cols.append(same & (j <= t))
    masks.append(j == t)
    end = same & (j > t)
    return [np.ascontiguousarray(a, np.float32) for a in (np.concatenate(cols, 1), end, np.concatenate(masks, 1))]


def layer(nc, x, ck, cv, state_in, norm1, w_in, w_a2, b_a2, qg, kg, gla_g, w_out, norm2, w_up, w_down,
          ident, diag_mask, sum_mats, end_mat, score_mask, y, new_k, new_v, new_state):
    def scratch(name, *shape):
        return nc.dram_tensor(name, shape, F32, kind="Internal").ap()

    qT = scratch("q_t", SB_HEADS, P, ROWS)
    kT = scratch("k_t", SB_HEADS, P, KEYS)
    gqk, gv = scratch("gla_qk", ROWS, 512), scratch("gla_v", ROWS, 512)
    sgate, la = scratch("gate", ROWS, 512), scratch("log_a", ROWS, 256)
    mix, h = scratch("mix", ROWS, D), scratch("h", ROWS, D)
    hTh, hTl = scratch("h_t_hi", KC, P, ROWS), scratch("h_t_lo", KC, P, ROWS)

    phase_project(nc, x, ck, norm1, w_in, w_a2, b_a2, qg, kg, ident, qT, kT, new_k, new_v, gqk, gv, sgate, la)
    with Pool(nc, "hd") as heads:
        operands = attention_operands(heads)
        phase_gla(nc, gqk, gv, sgate, la, gla_g, state_in, ident, sum_mats, end_mat, score_mask, mix, new_state,
                  operands[3][:, :, NEW_KEY_COL // P],
                  lambda sp, s_in, s_v: load_head(sp, operands, 0, 0, qT, kT, new_v, cv, s_in, s_v))
        with Pool(nc, "wo") as m:
            wh, wl = [m.sb(name, [P, 2, KC, 512], F32R) for name in ("wh", "wl")]
            phase_attention(nc, operands, qT, kT, new_v, cv, ident, diag_mask, mix, w_out, wh, wl)
            phase_output(nc, mix, x, wh, wl, norm2, ident, h, hTh, hTl)
    phase_mlp(nc, hTh, hTl, h, w_up, w_down, y)


def kernel(**inputs):
    import numpy as _np
    import concourse.bacc as _bacc
    from concourse import mybir as _mybir
    from concourse.bass_utils import run_bass_kernel_spmd as _run

    x = _np.concatenate([inputs["x_prompt"][0], inputs["x_sample"][0], _np.zeros((P - DEC, D), _np.float32)], 0)
    arrays = {"x": x, "cache_k": inputs["cache_sb_k"][0, 0], "cache_v": inputs["cache_sb_v"][0, 0].reshape(PAST, SB_HEADS * HD),
              "state_in": inputs["state_gla"][0, 0]}
    for name in ("norm1_g", "w_in", "w_a2", "b_a2", "q_norm_g", "k_norm_g", "gla_norm_g", "w_out", "norm2_g", "w_up", "w_down"):
        arrays[name] = inputs[name][0]
    arrays["b_a2"] = arrays["b_a2"].reshape(1, -1)
    sum_mats, end_mat, score_mask = gla_constants(_np)
    arrays["ident"] = _np.eye(P, dtype=_np.float32)
    k = _np.arange(P)
    arrays["diag_mask"] = _np.where(k[None, :] >= k[:, None], _np.float32(NEG), _np.float32(0)).astype(_np.float32)
    arrays["sum_mats"], arrays["end_mat"], arrays["score_mask"] = sum_mats, end_mat, score_mask

    nc = _bacc.Bacc("TRN2", target_bir_lowering=False, num_devices=1)
    arrays = {f"in_{name}": _np.ascontiguousarray(a) for name, a in arrays.items()}
    args = [nc.dram_tensor(name, a.shape, _mybir.dt.from_np(a.dtype), kind="ExternalInput").ap() for name, a in arrays.items()]
    outs = {"y": (SEQ + DEC, D), "new_k": (SEQ + DEC, 512), "new_v": (SEQ + DEC, 512), "new_state": (2, GLA_HEADS, DK, DV)}
    for name, shape in outs.items():
        args.append(nc.dram_tensor(f"out_{name}", shape, F32, kind="ExternalOutput").ap())
    layer(nc, *args)
    got = _run(nc, [arrays], core_ids=[0]).results[0]
    yy, nk, nv, st = [got[f"out_{name}"] for name in outs]

    def heads(a):
        return a.reshape(1, 1, -1, SB_HEADS, HD)

    return (yy[None, :SEQ], yy[None, SEQ:], heads(nk[:SEQ]), heads(nv[:SEQ]), st[0][None, None],
            heads(nk[SEQ:]), heads(nv[SEQ:]), st[1][None, None])
```
